# Optimizing a Trainium2 kernel written in Bass

```python
import math
import jax, jax.numpy as jnp
from jax import lax
import numpy as np

D_MODEL = 1024
BATCH = 1
SEQ = 128
DEPTH = 2
DEC_BATCH = 1
DEC_SEQ = 512
PAST_LEN = 128

GRID_W = 64
N_MIXERS = 2
N_DA = (DEPTH + 1) // 2
N_ML = DEPTH // 2
DA_HEADS = 8
DA_DK = 64
DA_DV = 2 * DA_DK
DA_QK = DA_HEADS * 2 * DA_DK
DA_V = DA_HEADS * DA_DV
ML_HEADS = 4
ML_DK = D_MODEL // 2 // ML_HEADS
ML_DV = D_MODEL // ML_HEADS
ML_QK = ML_HEADS * ML_DK
ML_V = ML_HEADS * ML_DV
ML_GATES = 2 * 2 * ML_HEADS
ML_IN = 2 * ML_QK + 2 * ML_V + ML_GATES
ML_CHUNK = 64
CONV_W = 3
D_FF = 2816
Q_BLOCK = 128
ROPE_THETA = 10000.0
ALPHA = (2 * DEPTH) ** 0.25
BETA = (8 * DEPTH) ** -0.25
EPS = 1e-5

kernel_name = 'hybrid_diffattn_mlstm_dit_step'

def layer_norm(x, g, b):
    xf = x.astype(jnp.float32)
    mu = jnp.mean(xf, axis=-1, keepdims=True)
    var = jnp.mean(jnp.square(xf - mu), axis=-1, keepdims=True)
    return ((xf - mu) * lax.rsqrt(var + EPS) * g + b).astype(x.dtype)

def post_norm(x, y, g, b):
    return layer_norm(ALPHA * x + y, g, b)

def modulate(x, shift, scale):
    return x * (1 + scale) + shift

def dwconv3(x, w, b):
    L = x.shape[1]
    xp = jnp.pad(x, ((0, 0), (1, 1), (0, 0)))
    return xp[:, :L] * w[0] + xp[:, 1:L + 1] * w[1] + xp[:, 2:] * w[2] + b

def conv_ffn(h, w_up, conv_w, conv_b, w_down):
    u = dwconv3(h @ w_up, conv_w, conv_b)
    g, val = jnp.split(u, 2, axis=-1)
    return (jax.nn.silu(g) * val) @ w_down

def rope_2d(x):
    L = x.shape[1]
    rows = L // GRID_W
    row = jnp.repeat(jnp.arange(rows), GRID_W).astype(jnp.float32)
    col = jnp.tile(jnp.arange(GRID_W), rows).astype(jnp.float32)
    half = DA_DK // 2
    nf = half // 2
    inv = ROPE_THETA ** (-jnp.arange(nf, dtype=jnp.float32) / nf)

    def rot(xa, pos):
        ang = pos[:, None] * inv[None, :]
        cos = jnp.cos(ang)[None, :, None, None, :]
        sin = jnp.sin(ang)[None, :, None, None, :]
        x1, x2 = xa[..., :nf], xa[..., nf:]
        return jnp.concatenate([x1 * cos - x2 * sin, x2 * cos + x1 * sin], axis=-1)

    xf = x.astype(jnp.float32)
    return jnp.concatenate([rot(xf[..., :half], row), rot(xf[..., half:], col)], axis=-1).astype(x.dtype)

def da_project(h, w_qkv):
    B, L, _ = h.shape
    q, k, v = jnp.split(h @ w_qkv, [DA_QK, 2 * DA_QK], axis=-1)
    return (q.reshape(B, L, DA_HEADS, 2, DA_DK), k.reshape(B, L, DA_HEADS, 2, DA_DK),
            v.reshape(B, L, DA_HEADS, DA_DV))

def da_lambda(lam, layer):
    lam_init = 0.8 - 0.6 * math.exp(-0.3 * layer)
    lf = lam.astype(jnp.float32)
    lam_full = jnp.exp(jnp.sum(lf[0] * lf[1])) - jnp.exp(jnp.sum(lf[2] * lf[3])) + lam_init
    return lam_full, lam_init

def diff_attend(q, k, v, lam):
    B, Lq = q.shape[:2]
    nb = Lq // Q_BLOCK
    qb = jnp.moveaxis(q.reshape(B, nb, Q_BLOCK, DA_HEADS, 2, DA_DK), 1, 0)
    scale = DA_DK ** -0.5

    def block(qi):
        s = jnp.einsum('bqhmd,bkhmd->bhmqk', qi, k).astype(jnp.float32) * scale
        p = jax.nn.softmax(s, axis=-1)
        a = (p[:, :, 0] - lam * p[:, :, 1]).astype(v.dtype)
        return jnp.einsum('bhqk,bkhd->bqhd', a, v)

    o = lax.map(block, qb)
    return jnp.moveaxis(o, 0, 1).reshape(B, Lq, DA_HEADS, DA_DV)

def da_output(o, subln_w, lam_init, w_o):
    B, L = o.shape[:2]
    of = o.astype(jnp.float32)
    of = of * lax.rsqrt(jnp.mean(jnp.square(of), axis=-1, keepdims=True) + EPS) * subln_w
    of = of * (1.0 - lam_init)
    return of.astype(o.dtype).reshape(B, L, DA_V) @ w_o

def ml_project(h, w_in, conv_w, conv_b, b_gate):
    B, L, _ = h.shape
    qk, v, o, gates = jnp.split(h @ w_in, [2 * ML_QK, 2 * ML_QK + ML_V, 2 * ML_QK + 2 * ML_V], axis=-1)
    qk = jax.nn.silu(dwconv3(qk, conv_w, conv_b))
    q, k = jnp.split(qk, 2, axis=-1)
    q = q.reshape(B, L, ML_HEADS, ML_DK).transpose(0, 2, 1, 3)
    k = k.reshape(B, L, ML_HEADS, ML_DK).transpose(0, 2, 1, 3) * (ML_DK ** -0.5)
    v = v.reshape(B, L, ML_HEADS, ML_DV).transpose(0, 2, 1, 3)
    gates = (gates + b_gate).astype(jnp.float32).reshape(B, L, 2, 2, ML_HEADS)
    gates = jnp.transpose(gates, (2, 3, 0, 4, 1))
    ig = gates[:, 0]
    lf = jax.nn.log_sigmoid(gates[:, 1])
    return q, k, v, o, ig, lf

def mlstm_scan(q, k, v, ig, lf, C0, n0, m0):
    B, H, L, _ = q.shape
    nc = L // ML_CHUNK

    def chunks(x):
        x = x.astype(jnp.float32).reshape((B, H, nc, ML_CHUNK) + x.shape[3:])
        return jnp.moveaxis(x, 2, 0)

    tril = jnp.tril(jnp.ones((ML_CHUNK, ML_CHUNK), dtype=bool))

    def step(carry, inp):
        C, n, m = carry
        qc, kc, vc, ic, fc = inp
        b = jnp.cumsum(fc, axis=-1)
        intra = jnp.where(tril, b[..., :, None] - b[..., None, :] + ic[..., None, :], -jnp.inf)
        inter = b + m[..., None]
        m_row = jnp.maximum(inter, jnp.max(intra, axis=-1))
        w_intra = jnp.exp(intra - m_row[..., None])
        w_inter = jnp.exp(inter - m_row)
        s = jnp.einsum('bhtd,bhsd->bhts', qc, kc) * w_intra
        num = w_inter[..., None] * jnp.einsum('bhtd,bhde->bhte', qc, C) + jnp.einsum('bhts,bhse->bhte', s, vc)
        den = w_inter * jnp.einsum('bhtd,bhd->bht', qc, n) + jnp.sum(s, axis=-1)
        h = num / jnp.maximum(jnp.abs(den), jnp.exp(-m_row))[..., None]
        b_last = b[..., -1]
        dec = b_last[..., None] - b + ic
        m_new = jnp.maximum(b_last + m, jnp.max(dec, axis=-1))
        w_s = jnp.exp(dec - m_new[..., None])
        carry_w = jnp.exp(b_last + m - m_new)
        C_new = carry_w[..., None, None] * C + jnp.einsum('bhs,bhsd,bhse->bhde', w_s, kc, vc)
        n_new = carry_w[..., None] * n + jnp.einsum('bhs,bhsd->bhd', w_s, kc)
        return (C_new, n_new, m_new), h

    carry0 = (C0.astype(jnp.float32), n0.astype(jnp.float32), m0.astype(jnp.float32))
    (C, n, m), h = lax.scan(step, carry0, (chunks(q), chunks(k), chunks(v), chunks(ig), chunks(lf)))
    h = jnp.moveaxis(h, 0, 2).reshape(B, H, L, ML_DV)
    return h, C, n, m

def ml_bidir(q, k, v, ig, lf, C0, n0, m0):
    hf, Cf, nf, mf = mlstm_scan(q, k, v, ig[0], lf[0], C0[:, 0], n0[:, 0], m0[:, 0])
    rev = lambda x: jnp.flip(x, axis=2)
    hb, Cb, nb, mb = mlstm_scan(rev(q), rev(k), rev(v), rev(ig[1]), rev(lf[1]), C0[:, 1], n0[:, 1], m0[:, 1])
    h = hf + rev(hb)
    return h, jnp.stack([Cf, Cb], axis=1), jnp.stack([nf, nb], axis=1), jnp.stack([mf, mb], axis=1)

def ml_output(h, o, norm_w, w_out):
    B, H, L, _ = h.shape
    mu = jnp.mean(h, axis=-1, keepdims=True)
    var = jnp.mean(jnp.square(h - mu), axis=-1, keepdims=True)
    hn = (h - mu) * lax.rsqrt(var + EPS) * norm_w.astype(jnp.float32)[:, None, :]
    hn = hn.transpose(0, 2, 1, 3).reshape(B, L, ML_V).astype(o.dtype)
    return (jax.nn.sigmoid(o) * hn) @ w_out

def setup_inputs(seed: int = 0) -> dict:
    key = jax.random.key(seed)
    ks = jax.random.split(key, 32)
    nrm = lambda k, shape, s: jax.random.normal(k, shape, jnp.float32) * s
    ada_b = jnp.concatenate([nrm(ks[6], (DEPTH, 2, 2 * D_MODEL), 0.02),
                             1.0 + nrm(ks[7], (DEPTH, 2, D_MODEL), 0.02)], axis=-1).reshape(DEPTH, 6 * D_MODEL)
    ib = nrm(ks[16], (N_ML, 2, 1, ML_HEADS), 0.1)
    fb = jnp.linspace(3.0, 6.0, ML_HEADS, dtype=jnp.float32)[None, None, None, :] + nrm(ks[17], (N_ML, 2, 1, ML_HEADS), 0.1)
    ml_b_gate = jnp.concatenate([ib, fb], axis=2).reshape(N_ML, ML_GATES)
    return {
        'x_prompt': nrm(ks[0], (BATCH, SEQ, D_MODEL), 1.0),
        'x_sample': nrm(ks[1], (DEC_BATCH, DEC_SEQ, D_MODEL), 1.0),
        'c': nrm(ks[2], (DEC_BATCH, D_MODEL), 1.0),
        'cache_k': nrm(ks[3], (DEC_BATCH, N_DA, PAST_LEN, DA_HEADS, 2, DA_DK), 1.0),
        'cache_v': nrm(ks[4], (DEC_BATCH, N_DA, PAST_LEN, DA_HEADS, DA_DV), 1.0),
        'state_C': nrm(ks[24], (DEC_BATCH, N_ML, 2, ML_HEADS, ML_DK, ML_DV), 0.5),
        'state_n': nrm(ks[25], (DEC_BATCH, N_ML, 2, ML_HEADS, ML_DK), 0.5),
        'state_m': nrm(ks[26], (DEC_BATCH, N_ML, 2, ML_HEADS), 1.0),
        'c_ctx': nrm(ks[5], (D_MODEL,), 1.0),
        'ada_w': nrm(ks[8], (DEPTH, D_MODEL, 6 * D_MODEL), 0.02),
        'ada_b': ada_b,
        'ln_g': 1.0 + nrm(ks[9], (DEPTH, 2, D_MODEL), 0.02),
        'ln_b': nrm(ks[10], (DEPTH, 2, D_MODEL), 0.02),
        'da_w_qkv': nrm(ks[11], (N_DA, D_MODEL, 2 * DA_QK + DA_V), D_MODEL ** -0.5),
        'da_lam': nrm(ks[12], (N_DA, 4, DA_DK), 0.1),
        'da_subln': 1.0 + nrm(ks[13], (N_DA, DA_DV), 0.02),
        'da_w_o': nrm(ks[14], (N_DA, DA_V, D_MODEL), BETA * DA_V ** -0.5),
        'ml_w_in': nrm(ks[15], (N_ML, D_MODEL, ML_IN), D_MODEL ** -0.5),
        'ml_conv_w': nrm(ks[18], (N_ML, CONV_W, 2 * ML_QK), 0.5),
        'ml_conv_b': nrm(ks[19], (N_ML, 2 * ML_QK), 0.02),
        'ml_b_gate': ml_b_gate,
        'ml_norm_w': 1.0 + nrm(ks[20], (N_ML, ML_HEADS, ML_DV), 0.02),
        'ml_w_out': nrm(ks[21], (N_ML, ML_V, D_MODEL), BETA * ML_V ** -0.5),
        'ffn_w_up': nrm(ks[22], (DEPTH, D_MODEL, 2 * D_FF), D_MODEL ** -0.5),
        'ffn_conv_w': nrm(ks[23], (DEPTH, CONV_W, 2 * D_FF), 0.5),
        'ffn_conv_b': nrm(ks[27], (DEPTH, 2 * D_FF), 0.02),
        'ffn_w_down': nrm(ks[28], (DEPTH, D_FF, D_MODEL), BETA * D_FF ** -0.5),
    }

def reference(x_prompt, x_sample, c, cache_k, cache_v, state_C, state_n, state_m, c_ctx,
              ada_w, ada_b, ln_g, ln_b, da_w_qkv, da_lam, da_subln, da_w_o,
              ml_w_in, ml_conv_w, ml_conv_b, ml_b_gate, ml_norm_w, ml_w_out,
              ffn_w_up, ffn_conv_w, ffn_conv_b, ffn_w_down):
    cond_p = jax.nn.silu(c_ctx)
    cond_s = jax.nn.silu(c)
    xp, xs = x_prompt, x_sample
    bp = x_prompt.shape[0]
    new_k, new_v, new_C, new_n, new_m = [], [], [], [], []
    for i in range(DEPTH):
        j = i // N_MIXERS
        mod_p = jnp.split(cond_p @ ada_w[i] + ada_b[i], 6, axis=-1)
        mod_s = jnp.split((cond_s @ ada_w[i] + ada_b[i])[:, None, :], 6, axis=-1)
        hp = modulate(xp, mod_p[0], mod_p[1])
        hs = modulate(xs, mod_s[0], mod_s[1])
        if i % N_MIXERS == 0:
            lam, lam_init = da_lambda(da_lam[j], i)
            qp, kp, vp = da_project(hp, da_w_qkv[j])
            yp = da_output(diff_attend(qp, kp, vp, lam), da_subln[j], lam_init, da_w_o[j])
            new_k.append(kp)
            new_v.append(vp)
            qs, ks_, vs = da_project(hs, da_w_qkv[j])
            k_all = jnp.concatenate([cache_k[:, j], rope_2d(ks_)], axis=1)
            v_all = jnp.concatenate([cache_v[:, j], vs], axis=1)
            ys = da_output(diff_attend(rope_2d(qs), k_all, v_all, lam), da_subln[j], lam_init, da_w_o[j])
        else:
            qp, kp, vp, op, igp, lfp = ml_project(hp, ml_w_in[j], ml_conv_w[j], ml_conv_b[j], ml_b_gate[j])
            zC = jnp.zeros((bp, 2, ML_HEADS, ML_DK, ML_DV), jnp.float32)
            zn = jnp.zeros((bp, 2, ML_HEADS, ML_DK), jnp.float32)
            zm = jnp.zeros((bp, 2, ML_HEADS), jnp.float32)
            hpm, Cp, npn, mpm = ml_bidir(qp, kp, vp, igp, lfp, zC, zn, zm)
            yp = ml_output(hpm, op, ml_norm_w[j], ml_w_out[j])
            new_C.append(Cp)
            new_n.append(npn)
            new_m.append(mpm)
            qs, ks_, vs, os_, igs, lfs = ml_project(hs, ml_w_in[j], ml_conv_w[j], ml_conv_b[j], ml_b_gate[j])
            hsm, _, _, _ = ml_bidir(qs, ks_, vs, igs, lfs, state_C[:, j], state_n[:, j], state_m[:, j])
            ys = ml_output(hsm, os_, ml_norm_w[j], ml_w_out[j])
        xp = post_norm(xp, mod_p[2] * yp, ln_g[i, 0], ln_b[i, 0])
        xs = post_norm(xs, mod_s[2] * ys, ln_g[i, 0], ln_b[i, 0])
        hp = modulate(xp, mod_p[3], mod_p[4])
        hs = modulate(xs, mod_s[3], mod_s[4])
        fp = conv_ffn(hp, ffn_w_up[i], ffn_conv_w[i], ffn_conv_b[i], ffn_w_down[i])
        fs = conv_ffn(hs, ffn_w_up[i], ffn_conv_w[i], ffn_conv_b[i], ffn_w_down[i])
        xp = post_norm(xp, mod_p[5] * fp, ln_g[i, 1], ln_b[i, 1])
        xs = post_norm(xs, mod_s[5] * fs, ln_g[i, 1], ln_b[i, 1])
    return (xp, xs, jnp.stack(new_k, axis=1), jnp.stack(new_v, axis=1), jnp.stack(new_C, axis=1), jnp.stack(new_n, axis=1), jnp.stack(new_m, axis=1))


_drawn_inputs = setup_inputs


def setup_inputs(seed=0):
    import zlib

    import numpy as np

    out = dict(_drawn_inputs(seed))
    spreads = {}
    factors = {'state_n': 5.782,
     'state_m': 3.403,
     'da_subln': 4.433,
     'ml_norm_w': 8.0,
     'ffn_conv_b': 5.196}
    for name, (base, spread) in spreads.items():
        noise = np.random.default_rng([zlib.crc32(name.encode()), seed]).standard_normal(out[name].shape)
        drawn = base * np.exp(spread * noise) if base else spread * noise
        out[name] = __import__('jax').numpy.asarray(drawn.astype(out[name].dtype))
    for name, factor in factors.items():
        out[name] = (out[name] * factor).astype(out[name].dtype)
    return out
```

```python
import math
from contextlib import ExitStack

import numpy as np

import concourse.bass as bass
from concourse import mybir

F32 = mybir.dt.float32
F32R = mybir.dt.float32r
ALU = mybir.AluOpType
ACT = mybir.ActivationFunctionType
AX = mybir.AxisListType

P = 128
D = 1024
KT = D // P
CTX, LAT = 128, 512
PAST = 128
C0, L0 = 1, CTX + 2
TP = 644
HALF = TP // 2
DFF = 2816
GH = DFF // P // 2
WMAX = GH * P
DA_HEADS, DK = 8, 64
ML_HEADS, MDK, MDV = 4, 128, 256
GRID_W = 64
DEPTH = 2
ALPHA = (2 * DEPTH) ** 0.25
EPS = 1e-5
LAM_INIT = 0.8 - 0.6 * math.exp(-0.3 * 0)
QSCALE = DK ** -0.5
KSCALE = MDK ** -0.5
NMOD = 6 * KT
AS = KT
NA = DEPTH * NMOD // AS
BUILD = 3

V_ADAB = 0
V_LNG = V_ADAB + DEPTH * NMOD
V_LNB = V_LNG + DEPTH * 2 * KT
V_FCW = V_LNB + DEPTH * 2 * KT
V_FCB = V_FCW + DEPTH * 2 * 3 * 2 * GH
V_MCW = V_FCB + DEPTH * 2 * 2 * GH
V_MCB = V_MCW + 3 * KT
V_SUB = V_MCB + KT
V_MNW = V_SUB + 1
V_N0 = V_MNW + KT
V_M0 = V_N0 + 2 * ML_HEADS
V_BG = V_M0 + 2 * ML_HEADS
V_LAM = V_BG + 16
V_COND = V_LAM + 4 * DK
NV = V_COND + 2 * KT

U_QKV = 0
U_WO = U_QKV + 3 * DA_HEADS
U_FFN0 = U_WO + KT
U_MLIN = U_FFN0 + 2 * (2 * GH + KT)
U_MLOUT = U_MLIN + 6 * ML_HEADS
U_FFN1 = U_MLOUT + KT
U_END = U_FFN1 + 2 * (2 * GH + KT)
MCOP = 3 * DA_HEADS + 4 * GH


PIECES = ((0, 0, L0 - 1, 0, 0), (0, L0 - 1, HALF, L0 - 1, 1), (1, 0, HALF, HALF, 1))
SPANS = ((C0, C0 + CTX, 0), (L0, L0 + LAT, 1))


def hybrid_step(nc, a, o):
    ctx = ExitStack()
    with ctx:
        def sb(name, shape, dt=F32, scope=ctx):
            return scope.enter_context(nc.sbuf_tensor(name, shape, dt))

        def ps(name, shape, scope=ctx):
            return scope.enter_context(nc.psum_tensor(name, shape, F32))

        def sem(name):
            return ctx.enter_context(nc.semaphore(name))

        X = sb("X", [P, KT, TP])
        Hh = sb("Hh", [P, KT, TP], F32R)
        Hl = sb("Hl", [P, KT, TP], F32R)
        wraw = [sb(f"wraw{k}", [P, WMAX]) for k in range(2)]
        whi = [sb(f"whi{k}", [P, WMAX], F32R) for k in range(2)]
        wlo = [sb(f"wlo{k}", [P, WMAX], F32R) for k in range(2)]
        vec = sb("vec", [P, NV])
        ident = sb("ident", [P, P])
        ones = sb("ones", [P, P])
        mean_w = sb("mean_w", [P, P])
        cond = sb("cond", [P, KT, 2])
        mods = sb("mods", [P, DEPTH * NMOD, 2])
        la = sb("la", [P, KT, 2])
        lb = sb("lb", [P, KT, 2])
        xa = sb("xa", [P, KT])
        xb = sb("xb", [P, KT])

        nst = sb("nst", [P, 2, ML_HEADS])
        mst = sb("mst", [P, 2, ML_HEADS])
        sx = sb("sx", [P, TP + 2])
        ss = sb("ss", [P, TP])
        rs = sb("rs", [P, 2, HALF])
        h32t = sb("h32t", [P, 2, TP])
        h32 = [h32t[:, k, :] for k in range(2)]

        with ExitStack() as s:
            sq = sb("sq", [P, KT, TP], F32, s)
        with ExitStack() as s:
            Gh = sb("Gh", [P, GH, TP], F32R, s)
            Gl = sb("Gl", [P, GH, TP], F32R, s)
            fus = [sb(f"fus{k}", [P, TP + 2], F32, s) for k in range(2)]
            fcv = [sb(f"fcv{k}", [P, TP], F32, s) for k in range(2)]
            fsg = sb("fsg", [P, TP], F32, s)
            fpr = sb("fpr", [P, TP], F32, s)
        with ExitStack() as s:
            awr = [sb(f"awr{k}", [P, 2, 512], F32, s) for k in range(AS)]
            ahi = [sb(f"ahi{k}", [P, 2, 512], F32R, s) for k in range(AS // 2)]
            alo = [sb(f"alo{k}", [P, 2, 512], F32R, s) for k in range(AS // 2)]
            arow = [sb(f"arow{k}", [4, 512], F32, s) for k in range(2)]
            condr = sb("condr", [P, KT, 4], F32R, s)
            pick = sb("pick", [P, 2], F32, s)
        with ExitStack() as s:
            O32 = sb("O32", [P, KT, TP], F32, s)
            v32 = sb("v32", [P, TP], F32, s)
            Qh = [sb(f"Qh{k}", [P, TP], F32R, s) for k in range(2)]
            Ql = [sb(f"Ql{k}", [P, TP], F32R, s) for k in range(2)]
            KW = TP - 2 + PAST
            Kh = [sb(f"Kh{k}", [P, KW], F32R, s) for k in range(2)]
            Kl = [sb(f"Kl{k}", [P, KW], F32R, s) for k in range(2)]
            Vh = [sb(f"Vh{k}", [P, 6, P], F32R, s) for k in range(2)]
            Vl = [sb(f"Vl{k}", [P, 6, P], F32R, s) for k in range(2)]
            pr = sb("pr", [P, 2, LAT + PAST], F32, s)
            Ah = sb("Ah", [P, 5, LAT], F32R, s)
            Al = sb("Al", [P, 5, LAT], F32R, s)
            Aph = sb("Aph", [P, CTX], F32R, s)
            Apl = sb("Apl", [P, CTX], F32R, s)
            rope = sb("rope", [P, 2, LAT], F32, s)
            ckv = sb("ckv", [P, 2, P], F32, s)
            perm = sb("perm", [P, P], F32, s)
            sm = sb("sm", [P, 16], F32, s)
            lam = sb("lam", [P, 8], F32, s)
            lamp = sb("lamp", [P, 2, DK], F32, s)

        with ExitStack() as s:
            O32m = sb("O32m", [P, KT, TP], F32, s)
            mQh = sb("mQh", [P, TP], F32R, s)
            mQl = sb("mQl", [P, TP], F32R, s)
            mKh = sb("mKh", [P, TP + P], F32R, s)
            mKl = sb("mKl", [P, TP + P], F32R, s)
            mVh = sb("mVh", [P, 5, MDV], F32R, s)
            mVl = sb("mVl", [P, 5, MDV], F32R, s)
            mCh = sb("mCh", [P, 2, MDV], F32R, s)
            mCl = sb("mCl", [P, 2, MDV], F32R, s)
            mAh = sb("mAh", [P, 6, 2 * P], F32R, s)
            mAl = sb("mAl", [P, 6, 2 * P], F32R, s)
            mAph = sb("mAph", [P, P], F32R, s)
            mApl = sb("mApl", [P, P], F32R, s)
            wgh = sb("wgh", [P, KT, 16], F32R, s)
            wgl = sb("wgl", [P, KT, 16], F32R, s)
            wgf = sb("wgf", [P, KT, 16], F32, s)
            c0 = sb("c0", [P, 2, MDV], F32, s)
            ab = sb("ab", [P, 2, 5 * P], F32, s)
            mW = sb("mW", [P, 2, LAT], F32, s)
            mA = sb("mA", [P, 6 * P], F32, s)
            dg = mA[:, 0:5 * P].rearrange("p (i t) -> p i t", i=5)
            mask = sb("mask", [P, 8 * P], F32, s)
            tri = sb("tri", [P, 2, P], F32, s)
            hO = sb("hO", [P, 2, TP], F32, s)
            sq2 = h32t
            sig = sb("sig", [P, 2, TP], F32, s)
            vc = sb("vc", [P, MDV + 2], F32, s)
            kw = sb("kw", [P, 2, P], F32, s)
            cst = c0
            gt = sb("gt", [P, 5, 16], F32, s)
            xf = sb("xf", [P, 5, 8], F32, s)
            lft = sb("lft", [P, 40], F32, s)
            lf = sb("lf", [P, 5, 8], F32, s)
            bs = sb("bs", [P, 48], F32, s)
            a5 = sb("a5", [P, 5, 8], F32, s)
            ah = sb("ah", [P, 5, 2], F32, s)
            bh = sb("bh", [P, 5, 2], F32, s)
            msm = sb("msm", [P, 24], F32, s)
            mdn = sb("mdn", [P, 12], F32, s)

        pj = [ps(f"pj{k}", [P, 2, 512]) for k in range(1)]
        with ExitStack() as s:
            pj.append(ps("pj1", [P, 2, 512], s))
            st_mu = ps("st_mu", [P, 2, 512], s)
            st_va = ps("st_va", [P, 2, 512], s)
        with ExitStack() as s:
            prow = [ps(f"prow{k}", [4, 512], s) for k in range(2)]
            pmod0 = ps("pmod0", [P, 2 * KT, 2], s)
            pmod1 = ps("pmod1", [P, DEPTH * NMOD, 2], s)
        with ExitStack() as s:
            psS = ps("psS", [P, 3 * 512], s)
            psT = ps("psT", [P, 2, 512], s)
            psO = ps("psO", [P, 512], s)
        with ExitStack() as s:
            mS = ps("mS", [P, 2, 512], s)
            mT = ps("mT", [P, 2, 512], s)
            mO = ps("mO", [P, 2, 512], s)

        vec_in, xin, const_in, perm_in, rope_in, ckv_in = (
            sem(n) for n in ("vec_in", "xin", "const_in", "perm_in", "rope_in", "ckv_in"))
        w_landed = [sem(f"w_landed{k}") for k in range(2)]
        w_hi, w_lo = sem("w_hi"), sem("w_lo")
        tile_done = sem("tile_done")
        pj_copied = sem("pj_copied")
        pj_added = sem("pj_added")
        aw_landed = [sem(f"aw_landed{k}") for k in range(AS)]
        aw_hi = sem("aw_hi")
        aw_lo = [sem("aw_lo_even"), sem("aw_lo_odd")]
        aw_used = sem("aw_used")
        row_copied, row_turned = sem("row_copied"), sem("row_turned")
        cond_hi, cond_ready, ones_ready = sem("cond_hi"), sem("cond_ready"), sem("ones_ready")
        h32_ready, h_hi, h_ready = sem("h32_ready"), sem("h_hi"), sem("h_ready")
        o_ready, x_ready = sem("o_ready"), sem("x_ready")
        sx_ready, mu_done, d_ready, sq_ready, ss_ready, va_done, sd_ready = (
            sem(n) for n in ("sx_ready", "mu_done", "d_ready", "sq_ready", "ss_ready", "va_done", "sd_ready"))
        conv_ready, silu_ready, prod_ready, g_hi, g_ready = (
            sem(n) for n in ("conv_ready", "silu_ready", "prod_ready", "g_hi", "g_ready"))
        out_done, y_ready = sem("out_done"), sem("y_ready")
        lam_prod, lam_exp = sem("lam_prod"), sem("lam_exp")
        sc_done, nmax_ready, exp_ready, att_ready = (sem(n) for n in ("sc_done", "nmax_ready", "exp_ready", "att_ready"))
        t_full, t_free = sem("t_full"), sem("t_free")
        at_hi = sem("at_hi")
        roped, qk_hi, qk_ready, v_hi = (sem(n) for n in ("roped", "qk_hi", "qk_ready", "v_hi"))
        kv_out = [sem("k_out"), sem("v_out")]
        ck_split, sc_part = sem("ck_split"), sem("sc_part")
        ckc_hi = sem("ckc_hi")
        o_full, o_free, osq_ready, onorm, o32_clear = (
            sem(n) for n in ("o_full", "o_free", "osq_ready", "onorm", "o32_clear"))
        (wg_in, tri_in, wgh_ready, wg_ready, ax_ready, ln_ready, lf_ready, mt_full,
         mt_free, dg_ready, ms_done, ma_ready, mk_ready, mm_ready, me_ready, mat_hi,
         mo_full, mo_free, msq_ready, mconv, msilu, mq_hi, mk_scaled, mc_hi,
         c0_in, c0_split, mv_hi, dw_ready, ws_ready, c_out, mout_done) = (
            sem(n) for n in (
                "wg_in", "tri_in", "wgh_ready", "wg_ready", "ax_ready", "ln_ready", "lf_ready", "mt_full",
                "mt_free", "dg_ready", "ms_done", "ma_ready", "mk_ready", "mm_ready", "me_ready", "mat_hi",
                "mo_full", "mo_free", "msq_ready", "mconv", "msilu", "mq_hi", "mk_scaled", "mc_hi",
                "c0_in", "c0_split", "mv_hi", "dw_ready", "ws_ready", "c_out", "mout_done"))
        block = ctx.enter_context(nc.Block())

        def U(v):
            return v // 2, v % 2

        def loop(eng, n, body):
            with eng.Fori(0, n) as i:
                body(i)

        @block.sync
        def _(sp):
            sp.dma_start(vec[:, :], a["vecs"]).then_inc(vec_in, 16)
            sp.dma_start(ident[:, :], a["mats"][:, 0]).then_inc(const_in, 16)

            def load(src, pair, k, width, first=False):
                if not first:
                    sp.wait_ge(w_lo, 2 * pair + k - 1)
                sp.dma_start(wraw[k][:, 0:width], src).then_inc(w_landed[k], 16)

            def load_mod():
                w = a["w_ada"]
                for u in range(AS):
                    sp.dma_start(awr[u][:, :, :].rearrange("p a n -> p (a n)"), w[u]).then_inc(aw_landed[u], 16)
                sp.dma_start(X[:, :, :], a["xT"]).then_inc(xin, 16)

                def body(i):
                    for k in range(AS):
                        sp.wait_ge(aw_lo[k % 2], AS // 2 * i + k // 2 + 1)
                        sp.dma_start(awr[k][:, :, :].rearrange("p a n -> p (a n)"), w[bass.ds(AS * i + AS + k, 1)].rearrange(
                            "a p n -> p (a n)")).then_inc(aw_landed[k], 16)
                loop(sp, NA - 1, body)

            def load_run(w, base, n, width, at=0):
                def body(i):
                    for k in range(2):
                        load(w[bass.ds(2 * i + k + at, 1)].rearrange("a p n -> p (a n)"), base // 2 + i, k, width)
                loop(sp, n // 2, body)

            load_mod()
            sp.dma_start(perm[:, :], a["mats"][:, 1]).then_inc(perm_in, 16)
            sp.dma_start(rope[:, :, :], a["rope"]).then_inc(rope_in, 16)
            for k in range(2):
                load(a["w_qkv"][k], 0, k, D, first=True)
            load_run(a["w_qkv"], 2, 3 * DA_HEADS - 2, D, at=2)
            load_run(a["w_wo"], U_WO, KT, D)

            def load_ffn(layer, base):
                for half in range(2):
                    b = base + half * (2 * GH + KT)
                    load_run(a["w_up"], b, 2 * GH, D, at=(2 * layer + half) * 2 * GH)
                    load_run(a["w_dn"], b + 2 * GH, KT, WMAX, at=(2 * layer + half) * KT)
            load_ffn(0, U_FFN0)
            load_run(a["w_mlin"], U_MLIN, 2, D)
            sp.wait_ge(h_ready, 2 * KT + 1)
            sp.dma_start(wgf[:, :, :], a["w_gate"]).then_inc(wg_in, 16)
            sp.dma_start(tri[:, :, :], a["mats"][:, 2:4]).then_inc(tri_in, 16)
            sp.dma_start(mask[:, 3 * P:5 * P].rearrange("p (a b) -> p a b", a=2), a["mats"][:, 4:6]).then_inc(tri_in, 16)
            load_run(a["w_mlin"], U_MLIN + 2, 6 * ML_HEADS - 2, D, at=2)
            load_run(a["w_mlout"], U_MLOUT, KT, D)
            load_ffn(1, U_FFN1)
            sp.dma_start(o["state_n"], nst[:, :, :].rearrange("p d h -> p (d h)")).then_inc(out_done, 16)
            sp.dma_start(o["state_m"].rearrange("(a c) -> a c", a=1), mst[0:1, :, :].rearrange("p d h -> p (d h)")).then_inc(out_done, 16)
            for j in range(KT):
                sp.wait_ge(y_ready, j + 1)
                sp.dma_start(o["yT"][:, j], X[:, j, :]).then_inc(out_done, 16)
            sp.wait_ge(out_done, 16 * (KT + 2))
            for w in range(2):
                sp.wait_ge(kv_out[w], 16 * DA_HEADS)
            sp.wait_ge(c_out, 32 * ML_HEADS)


        @block.gpsimd
        def _(pool):
            nc.gpsimd.memset(ones[:, :], 1.0)
            nc.gpsimd.memset(mean_w[:, :], 1.0 / D).then_inc(ones_ready, 1)

            def split_run(base, n, width):
                def body(i):
                    for k in range(2):
                        pool.wait_ge(w_hi, base + 2 * i + k + 1)
                        nc.gpsimd.tensor_tensor(wlo[k][:, 0:width], wraw[k][:, 0:width],
                                                whi[k][:, 0:width].bitcast(F32), ALU.subtract).then_inc(w_lo, 1)
                loop(pool, n // 2, body)

            def modulation(i):
                for k in range(0, AS, 2):
                    pool.wait_ge(aw_hi, AS * i + k + 1)
                    nc.gpsimd.tensor_tensor(alo[k % 4][:, :, :], awr[k][:, :, :], ahi[k % 4][:, :, :].bitcast(F32),
                                            ALU.subtract).then_inc(aw_lo[0], 1)
            loop(pool, NA, modulation)

            def split_ffn(base):
                for half in range(2):
                    b = base + half * (2 * GH + KT)
                    split_run(b + 2 * (1 - half), 2 * GH - 2 * (1 - half), D)
                    split_run(b + 2 * GH, KT, WMAX)

            def output_lo(src, h_inst):
                def body(j):
                    pool.wait_ge(h_hi, KT * h_inst + j + 1)
                    lo, x, hi = (t[:, bass.ds(j, 1), :].rearrange("p a t -> p (a t)") for t in (Hl, src, Hh))
                    nc.gpsimd.tensor_tensor(lo, x, hi.bitcast(F32), ALU.subtract).then_inc(o_ready, 1)
                loop(pool, KT, body)

            def residual(n):
                for j in range(KT):
                    pool.wait_ge(h32_ready, KT * (n + 1) + j + 1)
                    nc.gpsimd.tensor_scalar(X[:, j, :], X[:, j, :], xa[:, j:j + 1], xb[:, j:j + 1], ALU.mult,
                                            ALU.add).then_inc(x_ready, 1)

            split_run(U_QKV, 3 * DA_HEADS + 2, D)
            output_lo(O32, 1)
            split_run(U_WO + 2, KT, D)
            residual(0)
            split_ffn(U_FFN0)
            split_run(U_MLIN, 2, D)
            residual(1)
            split_run(U_MLIN + 2, 6 * ML_HEADS, D)
            output_lo(O32m, 4)
            split_run(U_MLOUT + 2, KT, D)
            residual(2)
            split_ffn(U_FFN1)


        @block.tensor
        def _(pe):
            mm = nc.tensor.matmul

            def tile(pair, k, ks, n_k=KT, src=None, pairs=1, read=None):
                v = 2 * pair + k
                hi, lo = src or (Hh, Hl)
                out = pj[k if pairs == 2 else 0]
                if ks[0] == 0:
                    pe.wait_ge(w_lo, v + 1)
                    if read is None and (not isinstance(v, int) or v > 0):
                        read = (pj_copied, v)
                    if read:
                        pe.wait_ge(*read)
                for j in ks:
                    wh, wl = whi[k][:, j * P:(j + 1) * P], wlo[k][:, j * P:(j + 1) * P]
                    for n, (w, x) in enumerate(((wh, hi), (wh, lo), (wl, hi))):
                        for c in range(2):
                            last = mm(out[:, c, 0:HALF], w, x[:, j, c * HALF:(c + 1) * HALF],
                                      start=(j == 0 and n == 0), stop=(j == n_k - 1 and n == 2))
                if ks[-1] == n_k - 1:
                    last.then_inc(tile_done, 1)

            FULL = range(KT)

            def first_pair(pair, n_k, ready, base, src=None, reads=((), ())):
                for j in range(n_k):
                    pe.wait_ge(ready, base + j + 1)
                    for k in range(2):
                        tile(pair, k, [j], n_k, src, pairs=2, read=reads[k])

            def modulation():
                pe.wait_ge(cond_ready, 1)

                def turn_rows(n, slot):
                    pe.wait_ge(row_copied, n + 1)
                    for q in range(4):
                        at = 4 * n + q
                        if isinstance(n, int):
                            out = (pmod0 if at < 2 * KT else pmod1)[:, at, :]
                        else:
                            out = pmod1[:, bass.ds(at, 1), :].rearrange("p a b -> p (a b)")
                        last = mm(out, arow[slot][:, q * P:(q + 1) * P], pick[0:4, :], start=True, stop=True)
                    last.then_inc(row_turned, 1)

                def body(i):
                    for c in range(2):
                        n = 2 * i + c
                        if not isinstance(i, int) or i > 0:
                            pe.wait_ge(row_copied, n - 1)
                        for kp in range(KT // 2):
                            k = KT // 2 * c + kp
                            pe.wait_ge(aw_lo[k % 2], AS // 2 * i + k // 2 + 1)
                            for r in range(2):
                                for part, w in enumerate((ahi[k % 4], alo[k % 4])):
                                    last = mm(prow[c][:, :], condr[:, 2 * kp + r, :], w[:, r, :],
                                              start=(kp + r + part == 0), stop=(kp == KT // 2 - 1 and r + part == 2))
                            last.then_inc(aw_used, 1)
                        if not isinstance(i, int) or n > 0:
                            turn_rows(n - 1, 1 - c)
                for i in range(3):
                    body(i)
                with pe.Fori(3, NA) as i:
                    body(i)
                turn_rows(2 * NA - 1, 1)

            def layer_norm_stats(n):
                pe.wait_ge(sx_ready, KT * (n + 1))
                if n:
                    pe.wait_ge(sd_ready, n)
                for c in range(2):
                    last = mm(st_mu[:, c, 0:HALF], mean_w[:, :], sx[:, c * HALF:(c + 1) * HALF], start=True, stop=True)
                last.then_inc(mu_done, 1)
                for c in range(2):
                    pe.wait_ge(ss_ready, 2 * n + c + 1)
                    mm(st_va[:, c, 0:HALF], mean_w[:, :], ss[:, c * HALF:(c + 1) * HALF],
                       start=True, stop=True).then_inc(va_done, 1)

            def ffn(layer, base, h_inst):
                for half in range(2):
                    b = base + half * (2 * GH + KT)

                    def up(i):
                        for k in range(2):
                            tile(b // 2 + i, k, FULL, pairs=2, read=(pj_copied, copied + 2 * i + k - 1))
                    copied, added = 3 * DA_HEADS + (2 * layer + half) * 2 * GH + layer * 6 * ML_HEADS, KT * (1 + 2 * layer + half + layer)
                    pe.wait_ge(pj_added, added + 2)
                    if half == 0:
                        first_pair(b // 2, KT, h_ready, KT * h_inst)
                    else:
                        up(0)
                    with pe.Fori(1, GH) as i:
                        up(i)

                    def down(i):
                        for k in range(2):
                            tile((b + 2 * GH) // 2 + i, k, range(GH), GH, (Gh, Gl), pairs=2, read=(pj_added, added + 2 * i + k + 1))
                    pe.wait_ge(pj_copied, copied + 2 * GH)
                    first_pair((b + 2 * GH) // 2, GH, g_ready, GH * (2 * layer + half), (Gh, Gl))
                    with pe.Fori(1, KT // 2) as i:
                        down(i)

            pe.wait_ge(ones_ready, 1)
            modulation()

            def unit(m, c):
                return 3 * m + c // 2, c % 2

            def scores(idx, h, par, i):
                if not isinstance(idx, int) or idx > 0:
                    pe.wait_ge(exp_ready, idx)
                if i == 4:
                    spans = [(0, C0, C0 + CTX, 0), (640, C0, C0 + CTX, 1)]
                    q0 = C0
                else:
                    spans = [(512, L0 + 512, KW, 0), (0, L0, L0 + 512, 0), (1024, L0 + 384, KW, 1), (640, L0, L0 + 384, 1)]
                    q0 = L0 + i * P
                for at, k0, k1, m in spans:
                    r = slice(DK * m, DK * (m + 1))
                    if i < 4 and at == 640:
                        pe.wait_ge(sc_part, 4 * h + i + 1)
                    for n, (q, kk) in enumerate(((Qh, Kh), (Qh, Kl), (Ql, Kh))):
                        last = mm(psS[:, at:at + k1 - k0], q[par][r, q0:q0 + P], kk[par][r, k0:k1],
                                  start=(n == 0), stop=(n == 2))
                    if i < 4 and at == 512:
                        last.then_inc(sc_part, 1)
                last.then_inc(sc_done, 1)

            def t_wait(use):
                if not isinstance(use, int) or use > 0:
                    pe.wait_ge(t_free, use)

            def turn(idx, use, i):
                pe.wait_ge(att_ready, idx + 1)
                t_wait(use)
                for c in range(1 if i == 4 else 5):
                    last = nc.tensor.transpose(psT[:, :, :].rearrange("p a b -> p (a b)")[:, c * P:(c + 1) * P],
                                               pr[:, 0, c * P:(c + 1) * P], ident[:, :])
                last.then_inc(t_full, 1)

            def swap(vt, use, src):
                pe.wait_ge(pj_copied, vt + 1)
                t_wait(use)
                mm(psT[:, 0, :], perm[:, :], src[:, L0:L0 + LAT], start=True, stop=True).then_inc(t_full, 1)

            def values_ctx(h, par):
                pe.wait_ge(t_free, 3 + 9 * h + 1)
                if not isinstance(h, int) or h > 0:
                    pe.wait_ge(o_free, 2 * h)
                for n, (v_, t_) in enumerate(((Vh, Aph), (Vh, Apl), (Vl, Aph))):
                    last = mm(psO[:, 0:CTX], v_[par][:, 5, :], t_[:, :], start=(n == 0), stop=(n == 2))
                last.then_inc(o_full, 1)

            def values_lat(h, par, use):
                pe.wait_ge(t_free, use + 1)
                pe.wait_ge(o_free, 2 * h + 1)
                for c in range(5):
                    for n, (v_, t_) in enumerate(((Vh, Ah), (Vh, Al), (Vl, Ah))):
                        last = mm(psO[:, :], v_[par][:, c, :], t_[:, c, :], start=(c == 0 and n == 0),
                                  stop=(c == 4 and n == 2))
                last.then_inc(o_full, 1)

            def rms(h, use):
                pe.wait_ge(osq_ready, h + 1)
                t_wait(use)
                for c in range(2):
                    last = mm(psT[:, c, 0:HALF], ones[:, :], ss[:, c * HALF:(c + 1) * HALF], start=True, stop=True)
                last.then_inc(t_full, 1)

            def turn_v(vt, use):
                pe.wait_ge(pj_copied, vt + 1)
                t_wait(use)
                for c in range(5):
                    col = L0 + c * P if c < 4 else C0
                    last = nc.tensor.transpose(psT[:, :, :].rearrange("p a b -> p (a b)")[:, c * P:(c + 1) * P],
                                               v32[:, col:col + P], ident[:, :])
                last.then_inc(t_full, 1)

            def step(m, par, first=False, last=False):
                h = 2 * m + par
                u = 3 + 9 * h
                n = 2 * m + 1 if par == 0 else 2 * m + 2
                vq = 6 * m + 3 * (par + 1)
                pq = [unit(m, 3 * (par + 1) + c) for c in range(3)]
                lo, hi = range(0, 4), range(4, 8)
                pe.wait_ge(qk_ready, 2 * h + 2)
                scores(5 * h, h, par, 4)
                if not last:
                    tile(*pq[0], lo)
                turn(5 * h, u, 4)
                scores(5 * h + 1, h, par, 0)
                if not last:
                    tile(*pq[0], hi)
                turn(5 * h + 1, u + 1, 0)
                scores(5 * h + 2, h, par, 1)
                values_ctx(h, par)
                if not last:
                    tile(*pq[1], lo)
                turn(5 * h + 2, u + 2, 1)
                scores(5 * h + 3, h, par, 2)
                if not last:
                    swap(vq, u + 3, h32[0])
                    tile(*pq[1], hi)
                e = 0 if last else 1
                turn(5 * h + 3, u + 3 + e, 2)
                scores(5 * h + 4, h, par, 3)
                if not last:
                    tile(*pq[2], lo)
                turn(5 * h + 4, u + 4 + e, 3)
                if not last:
                    swap(vq + 1, u + 6, h32[1])
                values_lat(h, par, u + 4 + e)
                if not last:
                    tile(*pq[2], hi)
                rms(h, u + 5 + 2 * e)
                if not last:
                    turn_v(vq + 2, u + 8)

            pe.wait_ge(h_ready, KT)
            tile(0, 0, FULL)
            pe.wait_ge(perm_in, 16)
            swap(0, 0, h32[0])
            tile(0, 1, FULL)
            swap(1, 1, h32[1])
            tile(1, 0, FULL)
            turn_v(2, 2)
            step(0, 0)
            step(0, 1)
            with pe.Fori(1, DA_HEADS // 2 - 1) as m:
                step(m, 0)
                step(m, 1)
            step(DA_HEADS // 2 - 1, 0)
            step(DA_HEADS // 2 - 1, 1, last=True)

            def project_out(base, n, copied, added):
                pe.wait_ge(pj_copied, copied)
                first_pair(base // 2, KT, o_ready, KT * n, reads=[(pj_added, added + k + 1) for k in range(2)])
                with pe.Fori(1, KT // 2) as i:
                    for k in range(2):
                        tile(base // 2 + i, k, FULL, pairs=2, read=(pj_added, added + 2 * i + k + 1))
            project_out(U_WO, 0, 3 * DA_HEADS, 0)
            layer_norm_stats(0)
            ffn(0, U_FFN0, 1)
            layer_norm_stats(1)
            ML0 = U_MLIN // 2

            def m_wait(use):
                if not isinstance(use, int) or use > 0:
                    pe.wait_ge(mt_free, use)

            flatT = mT[:, :, :].rearrange("p a b -> p (a b)")

            def gates():
                pe.wait_ge(wg_ready, 1)
                for i in range(5):
                    c0 = L0 + i * P if i < 4 else C0
                    for j in range(KT):
                        for n, (x, w) in enumerate(((Hh, wgh), (Hh, wgl), (Hl, wgh))):
                            last = mm(mT[:, 0, 16 * i:16 * i + 16], x[:, j, c0:c0 + P], w[:, j, :],
                                      start=(j == 0 and n == 0), stop=(j == KT - 1 and n == 2))
                last.then_inc(mt_full, 1)
                pe.wait_ge(lf_ready, 1)
                pe.wait_ge(tri_in, 32)
                for d in range(2):
                    dc = slice(4 * d, 4 * d + 4)
                    for i in range(5):
                        out = mT[:, 1, 8 * i + 4 * d:8 * i + 4 * d + 4]
                        before = [] if i == 4 else (range(i) if d == 0 else range(i + 1, 4))
                        for b in before:
                            mm(out, ones[:, :], lf[:, b, dc], start=(b == before[0]), stop=False)
                        mm(out, tri[:, d, :], lf[:, i, dc], start=(len(before) == 0), stop=True)
                mm(mT[:, 1, 40:48], ones[:, :], lf[:, 4, :], start=True, stop=True).then_inc(mt_full, 1)

            def rows(use, h, d):
                pe.wait_ge(dg_ready, 2 * h + d + 1)
                m_wait(use)
                dgf = dg[:, :, :].rearrange("p i t -> p (i t)")
                mm(flatT[:, 0:512], ones[:, :], dgf[:, 0:512], start=True, stop=True)
                mm(flatT[:, 512:640], ones[:, :], dgf[:, 512:640], start=True, stop=True).then_inc(mt_full, 1)

            def m_scores(h, s, i):
                pe.wait_ge(mk_ready, h + 1)
                if not isinstance(h, int) or h + s > 0:
                    pe.wait_ge(ma_ready, 5 * h + s)
                q0 = C0 if i == 4 else L0 + i * P
                spans = [(0, C0, C0 + CTX)] if i == 4 else [(0, L0, L0 + LAT), (512, L0 + LAT, L0 + LAT + P + 2)]
                for bank, (at, k0, k1) in enumerate(spans):
                    for n, (q, kk) in enumerate(((mQh, mKh), (mQh, mKl), (mQl, mKh))):
                        last = mm(mS[:, bank, 0:k1 - k0], q[:, q0:q0 + P], kk[:, k0:k1], start=(n == 0), stop=(n == 2))
                last.then_inc(ms_done, 1)

            def m_turn(use, h, s, i):
                pe.wait_ge(ma_ready, 5 * h + s + 1)
                m_wait(use)
                for c in range(1 if i == 4 else 6):
                    last = nc.tensor.transpose(flatT[:, c * P:(c + 1) * P], mA[:, c * P:(c + 1) * P], ident[:, :])
                last.then_inc(mt_full, 1)

            def m_turn_v(use, w, tile_no):
                pe.wait_ge(pj_copied, tile_no)
                m_wait(use)
                for c in range(5):
                    col = L0 + c * P if c < 4 else C0
                    last = nc.tensor.transpose(flatT[:, c * P:(c + 1) * P], hO[:, w, col:col + P], ident[:, :])
                last.then_inc(mt_full, 1)

            def m_turn_k(use):
                m_wait(use)
                nc.tensor.transpose(flatT[:, 0:P], h32[1][:, C0:C0 + CTX], ident[:, :]).then_inc(mt_full, 1)

            def m_values(h, part, use):
                pe.wait_ge(mt_free, use + 1)
                if not isinstance(h, int) or h + part > 0:
                    pe.wait_ge(mo_free, 3 * h + part)
                for w in range(2):
                    dv = slice(w * P, (w + 1) * P)
                    if part == 0:
                        terms = [(mVh[:, 4, dv], mVl[:, 4, dv], mAph[:, :], mApl[:, :])]
                    else:
                        terms = [(mVh[:, c, dv], mVl[:, c, dv], mAh[:, c, :], mAl[:, c, :]) for c in range(4)]
                        terms += [(mCh[:, d, dv], mCl[:, d, dv], mAh[:, 4 + d, :], mAl[:, 4 + d, :]) for d in range(2)]
                    for c, (vh, vl, th, tl) in enumerate(terms):
                        for n, (v_, t_) in enumerate(((vh, th), (vh, tl), (vl, th))):
                            last = mm(mO[:, w, 0:P if part == 0 else 2 * P], v_, t_, start=(c == 0 and n == 0),
                                      stop=(c == len(terms) - 1 and n == 2))
                last.then_inc(mo_full, 1)

            def m_states(use, h):
                m_wait(use)
                for d in range(2):
                    last = mm(mT[:, d, 0:MDV + 2], kw[:, d, :], vc[:, :], start=True, stop=True)
                last.then_inc(mt_full, 1)

            def m_sum(use, src, ready, count):
                pe.wait_ge(ready, count)
                m_wait(use)
                for c in range(2):
                    for w in range(2):
                        last = mm(mT[:, c, 0:HALF], ones[:, :], src[:, w, c * HALF:(c + 1) * HALF], start=(w == 0), stop=(w == 1))
                last.then_inc(mt_full, 1)

            def m_head(h):
                def unit(c):
                    return ML0 + 3 * h + c // 2, c % 2

                def mt(c, ks=FULL):
                    tile(*unit(c), ks, read=(pj_copied, MCOP + 6 * h + c))
                u = 2 + 13 * h
                lo, hi = range(0, 4), range(4, 8)
                mt(0)
                rows(u, h, 0)
                mt(1)
                rows(u + 1, h, 1)
                mt(2)
                m_scores(h, 0, 4)
                mt(3)
                m_turn(u + 2, h, 0, 4)
                m_scores(h, 1, 0)
                m_turn_v(u + 3, 0, MCOP + 6 * h + 3)
                m_turn_v(u + 4, 1, MCOP + 6 * h + 4)
                mt(4, lo)
                m_turn(u + 5, h, 1, 0)
                m_scores(h, 2, 1)
                mt(4, hi)
                m_turn(u + 6, h, 2, 1)
                m_scores(h, 3, 2)
                m_values(h, 0, u + 4)
                m_turn_k(u + 7)
                m_values(h, 1, u + 6)
                mt(5, lo)
                m_turn(u + 8, h, 3, 2)
                m_scores(h, 4, 3)
                m_states(u + 9, h)
                mt(5, hi)
                m_turn(u + 10, h, 4, 3)
                m_values(h, 2, u + 10)
                m_sum(u + 11, hO, mo_free, 3 * h + 3)
                m_sum(u + 12, sq2, msq_ready, h + 1)

            pe.wait_ge(h_ready, KT * 3)
            pe.wait_ge(pj_added, 2 + 3 * KT)
            gates()
            m_head(0)
            with pe.Fori(1, ML_HEADS) as h:
                m_head(h)
            project_out(U_MLOUT, 1, MCOP + 6 * ML_HEADS, 3 * KT)
            layer_norm_stats(2)
            ffn(1, U_FFN1, 3)
            layer_norm_stats(3)

        @block.scalar
        def _(act):
            fn = nc.scalar.activation

            def split(pair, k, width=D, guard=True):
                act.wait_ge(w_landed[k], 16 * (pair + 1))
                if guard:
                    act.wait_ge(tile_done, 2 * pair + k - 1)
                nc.scalar.copy(whi[k][:, 0:width], wraw[k][:, 0:width]).then_inc(w_hi, 1)

            def evac(pair, k, dst, pairs=1):
                act.wait_ge(tile_done, 2 * pair + k + 1)
                nc.scalar.copy(dst.rearrange("p (a b) -> p a b", a=2), pj[k if pairs == 2 else 0][:, :, 0:HALF]
                               ).then_inc(pj_copied, 1)

            def h_build(inst, n32):
                for j in range(KT):
                    act.wait_ge(h32_ready, KT * n32 + j + 1)
                    nc.scalar.copy(Hh[:, j, :], h32[j % 2][:, :]).then_inc(h_hi, 1)

            def layer_norm(n):
                for c in range(2):
                    act.wait_ge(d_ready, 2 * n + c + 1)
                    fn(sq[:, :, c * HALF:(c + 1) * HALF], X[:, :, c * HALF:(c + 1) * HALF], ACT.Square).then_inc(sq_ready, 1)
                act.wait_ge(va_done, 2 * n + 2)
                fn(rs[:, :, :], st_va[:, :, 0:HALF], ACT.Sqrt, bias=EPS).then_inc(sd_ready, 1)

            def out_tiles(base, width=D, last_width=D):
                def body(i):
                    for k in range(2):
                        split(base // 2 + i + 1, k, width)
                loop(act, KT // 2 - 1, body)
                if last_width:
                    for k in range(2):
                        split(base // 2 + KT // 2, k, last_width)

            def ffn(layer, base, last=False):
                for half in range(2):
                    b = base + half * (2 * GH + KT)
                    cnt = (2 * layer + half) * GH

                    def body(i, width=D):
                        if not isinstance(i, int) or cnt + i > 0:
                            act.wait_ge(conv_ready, 2 * cnt + 2 * i)
                        evac(b // 2 + i, 0, fus[0][:, 1:TP + 1], pairs=2)
                        split(b // 2 + i + 1, 0, width)
                        evac(b // 2 + i, 1, fus[1][:, 1:TP + 1], pairs=2)
                        split(b // 2 + i + 1, 1, width)
                        act.wait_ge(conv_ready, 2 * cnt + 2 * i + 1)
                        fn(fsg[:, :], fcv[0][:, :], ACT.Silu).then_inc(silu_ready, 1)
                        act.wait_ge(prod_ready, cnt + i + 1)
                        g = Gh[:, bass.ds(i, 1), :].rearrange("p a t -> p (a t)") if not isinstance(i, int) else Gh[:, i, :]
                        nc.scalar.copy(g, fpr[:, :]).then_inc(g_hi, 1)
                    body(0)
                    with act.Fori(1, GH - 1) as i:
                        body(i)
                    body(GH - 1, WMAX)
                    b += 2 * GH
                    out_tiles(b, WMAX, 0 if last and half else D)

            act.wait_ge(vec_in, 16)
            fn(cond[:, :, :].rearrange("p a b -> p (a b)"), vec[:, V_COND:V_COND + 2 * KT], ACT.Silu)
            act.drain()
            nc.scalar.copy(condr[:, :, 0:2], cond[:, :, :]).then_inc(cond_hi, 1)

            def modulation(i, build=False):
                for k in range(AS):
                    act.wait_ge(aw_landed[k], 16 * (i + 1))
                    if not isinstance(i, int) or AS * i + k >= 4:
                        act.wait_ge(aw_used, AS * i + k - 3)
                    nc.scalar.copy(ahi[k % 4][:, :, :], awr[k][:, :, :]).then_inc(aw_hi, 1)
                    if build and k == AS // 2 - 1:
                        act.wait_ge(h32_ready, i - (BUILD - 1))
                        nc.scalar.copy(Hh[:, bass.ds(i - BUILD, 1), :].rearrange("p a t -> p (a t)"), h32[0][:, :]
                                       ).then_inc(h_hi, 1)
            for i in range(BUILD):
                modulation(i)
            with act.Fori(BUILD, BUILD + KT) as i:
                modulation(i, build=True)
            modulation(NA - 1)
            split(0, 0, guard=False)

            def unit(m, c):
                return 3 * m + c // 2, c % 2

            def load_cache(h):
                if not isinstance(h, int) or h > 0:
                    act.wait_ge(ck_split, h)
                hs = bass.ds(h, 1) if not isinstance(h, int) else slice(h, h + 1)
                act.dma_start(ckv[:, 0, :], a["cache_kT"][hs].rearrange("a p n -> p (a n)")).then_inc(ckv_in, 16)
                act.dma_start(ckv[:, 1, :], a["cache_v"][hs].rearrange("a p n -> p (a n)")).then_inc(ckv_in, 16)

            def exps(idx, i):
                act.wait_ge(nmax_ready, idx + 1)
                w = CTX if i == 4 else LAT + PAST
                for m in range(2):
                    last = fn(pr[:, m, 0:w], psS[:, 640 * m:640 * m + w], ACT.Exp, bias=sm[:, 2 + m:3 + m], scale=QSCALE,
                              accum_out=sm[:, 4 + m:5 + m])
                last.then_inc(exp_ready, 1)

            def turned(use, i):
                act.wait_ge(t_full, use + 1)
                if i == 4:
                    nc.scalar.copy(Aph[:, :], psT[:, 0, 0:CTX]).then_inc(at_hi, 1)
                else:
                    nc.scalar.copy(Ah[:, :, i * P:(i + 1) * P], psT[:, :, :].rearrange("p a b -> p (a b)")[:, 0:5 * P].rearrange(
                        "p (c q) -> p c q", c=5)).then_inc(at_hi, 1)

            def copy_kv(pu, h, which, dst):
                if not isinstance(h, int) or h > 0:
                    act.wait_ge(kv_out[which], 16 * h)
                    if which == 0:
                        act.wait_ge(qk_ready, 2 * h)
                evac(*pu, dst[:, :])
                act.drain()
                o_ = o["cache_kT"] if which == 0 else o["cache_vT"]
                hs = bass.ds(h, 1) if not isinstance(h, int) else slice(h, h + 1)
                act.dma_start(o_[hs].rearrange("a p n -> p (a n)"), dst[:, C0:C0 + CTX]).then_inc(kv_out[which], 16)

            def q_hi(n, par):
                act.wait_ge(roped, 2 * n + 1)
                nc.scalar.copy(Qh[par][:, :], h32[0][:, :]).then_inc(qk_hi, 1)

            def cache_hi(n, par):
                act.wait_ge(ckv_in, 32 * (n + 1))
                nc.scalar.copy(Kh[par][:, L0 + LAT:KW], ckv[:, 0, :])
                nc.scalar.copy(Vh[par][:, 4, :], ckv[:, 1, :]).then_inc(ckc_hi, 1)

            def k_hi(n, par):
                act.wait_ge(roped, 2 * n + 2)
                nc.scalar.copy(Kh[par][:, 0:L0 + LAT], h32[1][:, 0:L0 + LAT]).then_inc(qk_hi, 1)

            def values_hi(use, par):
                act.wait_ge(t_full, use + 1)
                t = psT[:, :, :].rearrange("p a b -> p (a b)")[:, 0:5 * P].rearrange("p (c q) -> p c q", c=5)
                nc.scalar.copy(Vh[par][:, 0:4, :], t[:, 0:4, :])
                nc.scalar.copy(Vh[par][:, 5, :], t[:, 4, :]).then_inc(v_hi, 1)

            def o_tile(h):
                return O32[:, bass.ds(h, 1), :].rearrange("p a t -> p (a t)") if not isinstance(h, int) else O32[:, h, :]

            def output_hi(src, done, tiles, per=1):
                for j in tiles:
                    act.wait_ge(done, j // per + 1)
                    nc.scalar.copy(Hh[:, j, :], src[:, j, :]).then_inc(h_hi, 1)

            def o_out(h, span, w):
                act.wait_ge(o_full, 2 * h + w + 1)
                nc.scalar.copy(o_tile(h)[:, span[0]:span[1]], psO[:, 0:span[1] - span[0]]).then_inc(o_free, 1)

            def step(m, par, last=False):
                h = 2 * m + par
                u = 3 + 9 * h
                n = h + 1
                e = 0 if last else 1
                pq = [unit(m, 3 * (par + 1) + c) for c in range(4)]
                exps(5 * h, 4)
                if not last:
                    load_cache(n)
                    split(*pq[1])
                else:
                    split(U_WO // 2, 1)
                    act.wait_ge(tile_done, 3 * DA_HEADS)
                    output_hi(O32, onorm, (0, 1))
                turned(u, 4)
                exps(5 * h + 1, 0)
                turned(u + 1, 0)
                if not last:
                    act.wait_ge(qk_ready, 2 * n - 1)
                    evac(*pq[0], h32[0][:, :])
                else:
                    output_hi(O32, onorm, (2, 3))
                exps(5 * h + 2, 1)
                o_out(h, (C0, C0 + CTX), 0)
                turned(u + 2, 1)
                if not last:
                    split(*pq[2])
                else:
                    output_hi(O32, onorm, (4, 5))
                exps(5 * h + 3, 2)
                if not last:
                    q_hi(n, 1 - par)
                    copy_kv(pq[1], n, 0, h32[1])
                turned(u + 3 + e, 2)
                exps(5 * h + 4, 3)
                if not last:
                    split(*pq[3])
                else:
                    output_hi(O32, onorm, (6,))
                turned(u + 4 + e, 3)
                if not last:
                    cache_hi(n, 1 - par)
                    k_hi(n, 1 - par)
                o_out(h, (L0, L0 + LAT), 1)
                act.drain()
                fn(ss[:, :], o_tile(h), ACT.Square).then_inc(osq_ready, 1)
                if not last:
                    copy_kv(pq[2], n, 1, v32)
                act.wait_ge(t_full, u + 6 + 2 * e - (0))
                fn(rs[:, :, :], psT[:, :, 0:HALF], ACT.Sqrt, scale=1.0 / P, bias=EPS).then_inc(t_free, 1)
                if not last:
                    values_hi(u + 8, 1 - par)

            act.wait_ge(lam_prod, 1)
            fn(lam[:, 2:4], lam[:, 0:2], ACT.Exp).then_inc(lam_exp, 1)
            load_cache(0)
            split(0, 1, guard=False)
            evac(0, 0, h32[0][:, :])
            split(1, 0)
            q_hi(0, 0)
            copy_kv((0, 1), 0, 0, h32[1])
            split(1, 1)
            cache_hi(0, 0)
            k_hi(0, 0)
            copy_kv((1, 0), 0, 1, v32)
            values_hi(2, 0)
            step(0, 0)
            step(0, 1)
            with act.Fori(1, DA_HEADS // 2 - 1) as m:
                step(m, 0)
                step(m, 1)
            step(DA_HEADS // 2 - 1, 0)
            step(DA_HEADS // 2 - 1, 1, last=True)
            output_hi(O32, onorm, (KT - 1,))
            out_tiles(U_WO)
            layer_norm(0)
            h_build(2, 1)
            ffn(0, U_FFN0, last=False)
            layer_norm(1)
            h_build(3, 2)
            act.wait_ge(wg_in, 16)
            nc.scalar.copy(wgh[:, :, :], wgf[:, :, :]).then_inc(wgh_ready, 1)
            act.wait_ge(ax_ready, 1)
            fn(lft[:, :], lft[:, :], ACT.Exp, scale=-1.0)
            act.drain()
            fn(lft[:, :], lft[:, :], ACT.Ln, bias=1.0).then_inc(ln_ready, 1)

            def m_exps(n, i):
                act.wait_ge(mm_ready, n + 1)
                spans = [(0, P), (0, P)] if i == 4 else [(0, (i + 1) * P), (i * P, LAT)]
                for d, (c0_, c1_) in enumerate(spans):
                    fn(mW[:, d, c0_:c1_], mW[:, d, c0_:c1_], ACT.Exp, bias=msm[:, 2 + d:3 + d])
                fn(msm[:, 8:12], msm[:, 4:8], ACT.Exp).then_inc(me_ready, 1)

            def m_turned(use, i):
                act.wait_ge(mt_full, use + 1)
                t = mT[:, :, :].rearrange("p a b -> p (a b)")
                if i == 4:
                    nc.scalar.copy(mAph[:, :], t[:, 0:P]).then_inc(mat_hi, 1)
                else:
                    c = (i % 2) * P
                    nc.scalar.copy(mAh[:, :, c:c + P], t[:, 0:6 * P].rearrange("p (c q) -> p c q", c=6)).then_inc(mat_hi, 1)

            def m_out(h, part):
                act.wait_ge(mo_full, 3 * h + part + 1)
                at, w = (C0, P) if part == 0 else (L0 + (part - 1) * 2 * P, 2 * P)
                nc.scalar.copy(hO[:, :, at:at + w], mO[:, :, 0:w]).then_inc(mo_free, 1)

            def m_head(h):
                def unit(c):
                    return U_MLIN // 2 + 3 * h + c // 2, c % 2

                def mevac(c, dst):
                    evac(*unit(c), dst)
                u = 2 + 13 * h
                if not isinstance(h, int):
                    split(*unit(1))
                    act.wait_ge(mconv, 2 * h)
                mevac(0, sx[:, 1:TP + 1])
                if not isinstance(h, int):
                    act.wait_ge(c_out, 32 * h)
                act.dma_start(c0[:, :, :], a["state_C"][:, bass.ds(h, 1)].rearrange("p a d n -> p (a d) n")).then_inc(c0_in, 16)
                act.wait_ge(mt_full, u + 1)
                flat = mT[:, :, :].rearrange("p a b -> p (a b)")
                nc.scalar.copy(ab[:, 0, :], flat[:, 0:640]).then_inc(mt_free, 1)
                act.wait_ge(mconv, 2 * h + 1)
                fn(h32[0][:, :], h32[0][:, :], ACT.Silu).then_inc(msilu, 1)
                split(*unit(2))
                mevac(1, sx[:, 1:TP + 1])
                split(*unit(3))
                act.drain()
                act.wait_ge(mt_full, u + 2)
                nc.scalar.copy(ab[:, 1, :], flat[:, 0:640]).then_inc(mt_free, 1)
                nc.scalar.copy(mQh[:, :], h32[0][:, :]).then_inc(mq_hi, 1)
                act.wait_ge(mconv, 2 * h + 2)
                fn(h32[1][:, :], h32[1][:, :], ACT.Silu).then_inc(msilu, 1)
                act.wait_ge(mk_scaled, h + 1)
                nc.scalar.copy(mKh[:, 0:TP - 2], h32[1][:, 0:TP - 2])
                nc.scalar.copy(mKh[:, TP - 2 + P:TP + P], msm[:, 20:22]).then_inc(mq_hi, 1)
                m_exps(5 * h, 4)
                if not isinstance(h, int):
                    act.wait_ge(mout_done, h)
                mevac(2, hO[:, 0, :])
                split(*unit(4))
                mevac(3, hO[:, 1, :])
                m_turned(u + 2, 4)
                m_exps(5 * h + 1, 0)
                for w in range(2):
                    act.wait_ge(mt_full, u + 4 + w)
                    t = flat[:, 0:5 * P].rearrange("p (c q) -> p c q", c=5)
                    nc.scalar.copy(vc[:, w * P:(w + 1) * P], t[:, 4, :])
                    nc.scalar.copy(mVh[:, :, w * P:(w + 1) * P], t).then_inc(mv_hi, 1)
                act.wait_ge(c0_in, 16 * (h + 1))
                nc.scalar.copy(mCh[:, :, :], c0[:, :, :]).then_inc(mc_hi, 1)
                split(*unit(5))
                m_turned(u + 5, 0)
                m_exps(5 * h + 2, 1)
                act.wait_ge(tile_done, U_MLIN + 6 * h + 5)
                fn(sig[:, 0, :].rearrange("p (a b) -> p a b", a=2), pj[0][:, :, 0:HALF], ACT.Sigmoid).then_inc(pj_copied, 1)
                m_turned(u + 6, 1)
                m_exps(5 * h + 3, 2)
                m_out(h, 0)
                act.wait_ge(dw_ready, h + 1)
                fn(msm[:, 16:18], msm[:, 14:16], ACT.Exp).then_inc(ws_ready, 1)
                m_out(h, 1)
                split(*unit(6))
                m_turned(u + 8, 2)
                m_exps(5 * h + 4, 3)
                act.wait_ge(mt_full, u + 10)
                act.wait_ge(c0_split, h + 1)
                nc.scalar.copy(nst[:, :, bass.ds(h, 1)], mT[:, :, MDV:MDV + 1])
                nc.scalar.copy(cst[:, :, :], mT[:, :, 0:MDV]).then_inc(mt_free, 1)
                act.drain()
                for d in range(2):
                    act.dma_start(o["state_C"][bass.ds(4 * d + h, 1)].rearrange("a p n -> p (a n)"), cst[:, d, :]).then_inc(c_out, 16)
                act.wait_ge(tile_done, U_MLIN + 6 * h + 6)
                fn(sig[:, 1, :].rearrange("p (a b) -> p a b", a=2), pj[0][:, :, 0:HALF], ACT.Sigmoid).then_inc(pj_copied, 1)
                m_turned(u + 10, 3)
                m_out(h, 2)
                act.wait_ge(mt_free, u + 12)
                fn(sq2[:, :, :], hO[:, :, :], ACT.Square).then_inc(msq_ready, 1)
                act.wait_ge(mt_full, u + 13)
                fn(rs[:, :, :], mT[:, :, 0:HALF], ACT.Sqrt, scale=1.0 / MDV, bias=EPS).then_inc(mt_free, 1)

            m_head(0)
            with act.Fori(1, ML_HEADS) as h:
                m_head(h)
            split(U_MLOUT // 2, 1)
            output_hi(O32m, mout_done, range(KT), per=2)
            out_tiles(U_MLOUT)
            layer_norm(2)
            h_build(5, 3)
            ffn(1, U_FFN1, last=True)
            layer_norm(3)

        @block.vector
        def _(dve):
            tt, ts, stt = nc.vector.tensor_tensor, nc.vector.tensor_scalar, nc.vector.scalar_tensor_tensor

            def col(i, n=1):
                return vec[:, bass.ds(i, n)] if not isinstance(i, int) else vec[:, i:i + n]

            def add_bias(pm, t0, t1):
                b = vec[:, V_ADAB + t0:V_ADAB + t1]
                tt(mods[:, t0:t1, :], pm[:, t0:t1, :], b[:, :, None].to_broadcast([P, t1 - t0, 2]), ALU.add)
                dve.drain()

            def copy_rows(n, slot):
                dve.wait_ge(aw_used, KT // 2 * (n + 1))
                if not isinstance(n, int) or n > 1:
                    dve.wait_ge(row_turned, n - 1)
                nc.vector.tensor_copy(arow[slot][:, :], prow[slot][:, :]).then_inc(row_copied, 1)

            def modulation(i, build=False):
                if build:
                    x = X[:, bass.ds(i - BUILD, 1), :].rearrange("p a t -> p (a t)")
                    hl, hh = (h[:, bass.ds(i - BUILD, 1), :].rearrange("p a t -> p (a t)") for h in (Hl, Hh))
                for k in range(1, AS, 2):
                    dve.wait_ge(aw_hi, AS * i + k + 1)
                    tt(alo[k % 4][:, :, :], awr[k][:, :, :], ahi[k % 4][:, :, :].bitcast(F32), ALU.subtract).then_inc(aw_lo[1], 1)
                    if k == 1 and build:
                        for t0, t1, m in SPANS:
                            last = ts(h32[0][:, t0:t1], x[:, t0:t1], la[:, bass.ds(i - BUILD, 1), m],
                                      lb[:, bass.ds(i - BUILD, 1), m], ALU.mult, ALU.add)
                        last.then_inc(h32_ready, 1)
                        dve.drain()
                    if k == 3 and (not isinstance(i, int) or i > 0):
                        copy_rows(2 * i - 1, 1)
                    if k == 5 and build:
                        ts(x, x, ALPHA, None, ALU.mult)
                copy_rows(2 * i, 0)
                if build:
                    dve.wait_ge(h_hi, i - (BUILD - 1))
                    tt(hl, h32[0][:, :], hh.bitcast(F32), ALU.subtract).then_inc(h_ready, 1)
                    dve.drain()

            def mod(layer, which):
                at = layer * NMOD + which * KT
                return mods[:, at:at + KT, :]

            def coefficients(ln, shift=None, scale=None):
                at = (2 * ln[0] + ln[1]) * KT
                g, b = vec[:, V_LNG + at:V_LNG + at + KT], vec[:, V_LNB + at:V_LNB + at + KT]
                if shift is None:
                    ts(xa[:, :], g, 1.0, None, ALU.mult)
                    ts(xb[:, :], b, 1.0, None, ALU.mult)
                    dve.drain()
                    return
                ts(xa[:, :], g, ALPHA, None, ALU.mult)
                ts(xb[:, :], b, ALPHA, None, ALU.mult)
                ts(la[:, :, :], scale, 1.0, None, ALU.add)
                dve.drain()
                tt(lb[:, :, :], la[:, :, :], b[:, :, None].to_broadcast([P, KT, 2]), ALU.mult)
                dve.drain()
                tt(lb[:, :, :], lb[:, :, :], shift, ALU.add)
                tt(la[:, :, :], la[:, :, :], g[:, :, None].to_broadcast([P, KT, 2]), ALU.mult)
                dve.drain()

            def clear_pads(t):
                nc.vector.memset(t[:, 0:C0], 0.0)
                nc.vector.memset(t[:, C0 + CTX:L0], 0.0)
                nc.vector.memset(t[:, L0 + LAT:TP], 0.0)

            def h_build(inst):
                for k in range(2):
                    clear_pads(h32[k])
                dve.drain()

                def lo(j):
                    dve.wait_ge(h_hi, KT * inst + j + 1)
                    tt(Hl[:, j, :], h32[j % 2][:, :], Hh[:, j, :].bitcast(F32), ALU.subtract).then_inc(h_ready, 1)
                for j in range(KT):
                    if j >= 2:
                        lo(j - 2)
                    dve.drain()
                    for t0, t1, m in SPANS:
                        last = ts(h32[j % 2][:, t0:t1], X[:, j, t0:t1], la[:, j, m:m + 1], lb[:, j, m:m + 1],
                                  ALU.mult, ALU.add)
                    last.then_inc(h32_ready, 1)
                lo(KT - 2)
                lo(KT - 1)

            def gated(base, gate, pairs_of, acc, n):
                if acc:
                    nc.vector.memset(sx[:, :], 0.0)
                    dve.drain()

                def body(i):
                    for k in range(2):
                        dve.wait_ge(tile_done, base + 2 * i + k + 1)
                        for bank, c0, c1, at, m in PIECES:
                            x = X[:, bass.ds(2 * i + k, 1), at:at + c1 - c0].rearrange("p a t -> p (a t)")
                            gt = mods[:, bass.ds(gate + 2 * i + k, 1), m]
                            last = stt(out=x, in0=pj[k][:, bank, c0:c1], scalar=gt, in1=x, op0=ALU.mult, op1=ALU.add)
                        last.then_inc(pj_added, 1)
                        dve.drain()
                        if acc:
                            tt(sx[:, 0:TP], sx[:, 0:TP], X[:, bass.ds(2 * i + k, 1), :].rearrange("p a t -> p (a t)"),
                               ALU.add).then_inc(sx_ready, 1)
                            dve.drain()
                loop(dve, KT // 2, body)

            def layer_norm(n):
                dve.wait_ge(mu_done, n + 1)
                for c in range(2):
                    x = X[:, :, c * HALF:(c + 1) * HALF]
                    tt(x, x, st_mu[:, c:c + 1, 0:HALF].to_broadcast([P, KT, HALF]), ALU.subtract).then_inc(d_ready, 1)
                for c in range(2):
                    dve.wait_ge(sq_ready, 2 * n + c + 1)
                    nc.vector.tensor_reduce(ss[:, c * HALF:(c + 1) * HALF], sq[:, :, c * HALF:(c + 1) * HALF].rearrange(
                        "p j t -> p t j"), AX.X, ALU.add).then_inc(ss_ready, 1)
                dve.wait_ge(sd_ready, n + 1)
                nc.vector.reciprocal(rs[:, :, :], rs[:, :, :])
                dve.drain()
                for c in range(2):
                    x = X[:, :, c * HALF:(c + 1) * HALF]
                    tt(x, x, rs[:, c:c + 1, :].to_broadcast([P, KT, HALF]), ALU.mult)
                dve.drain()

            def ffn(layer, base):
                for k in range(2):
                    nc.vector.memset(fus[k][:, 0:1], 0.0)
                    nc.vector.memset(fus[k][:, TP + 1:TP + 2], 0.0)
                dve.drain()
                for half in range(2):
                    b = base + half * (2 * GH + KT)
                    cnt = (2 * layer + half) * GH
                    w0 = V_FCW + (2 * layer + half) * 3 * 2 * GH
                    b0 = V_FCB + (2 * layer + half) * 2 * GH
                    copied = 3 * DA_HEADS + layer * 6 * ML_HEADS + 2 * cnt

                    def body(i):
                        for k in range(2):
                            f, c = fus[k], fcv[k]
                            dve.wait_ge(pj_copied, copied + 2 * i + k + 1)
                            tap = [col(w0 + 2 * GH * t + 2 * i + k) for t in range(3)]
                            ts(c[:, :], f[:, 1:TP + 1], tap[1], col(b0 + 2 * i + k), ALU.mult, ALU.add)
                            dve.drain()
                            stt(out=c[:, :], in0=f[:, 0:TP], scalar=tap[0], in1=c[:, :], op0=ALU.mult, op1=ALU.add)
                            dve.drain()
                            stt(out=c[:, :], in0=f[:, 2:TP + 2], scalar=tap[2], in1=c[:, :], op0=ALU.mult,
                                op1=ALU.add).then_inc(conv_ready, 1)
                        dve.drain()
                        dve.wait_ge(silu_ready, cnt + i + 1)
                        tt(fpr[:, :], fsg[:, :], fcv[1][:, :], ALU.mult).then_inc(prod_ready, 1)
                        dve.drain()
                        dve.wait_ge(g_hi, cnt + i + 1)
                        gh, gl = (g[:, bass.ds(i, 1), :].rearrange("p a t -> p (a t)") for g in (Gh, Gl))
                        tt(gl, fpr[:, :], gh.bitcast(F32), ALU.subtract).then_inc(g_ready, 1)
                    loop(dve, GH, body)
                    if half == 0:
                        dve.wait_ge(x_ready, KT * (2 * layer + 1))
                    gated(b + 2 * GH, layer * NMOD + 5 * KT, 2, half == 1, None)

            nc.vector.memset(xa[:, :], 0.0).then_inc(pj_added, 1)
            nc.vector.memset(xb[:, :], 0.0).then_inc(pj_added, 1)
            dve.wait_ge(const_in, 16)
            tt(pick[:, :], ident[:, 0:2], ident[:, 2:4], ALU.add)
            dve.wait_ge(cond_hi, 1)
            tt(condr[:, :, 2:4], cond[:, :, :], condr[:, :, 0:2].bitcast(F32), ALU.subtract).then_inc(cond_ready, 1)
            clear_pads(h32[0])
            for i in range(BUILD):
                modulation(i)
            dve.wait_ge(row_turned, 2 * KT // 4)
            add_bias(pmod0, 0, 2 * KT)
            ts(la[:, :, :], mod(0, 1), 1.0, None, ALU.add)
            ts(lb[:, :, :], mod(0, 0), 1.0, None, ALU.mult)
            dve.wait_ge(xin, 16)
            dve.drain()
            with dve.Fori(BUILD, BUILD + KT) as i:
                modulation(i, build=True)
            modulation(NA - 1)
            copy_rows(2 * NA - 1, 1)
            dve.wait_ge(row_turned, 2 * NA)
            add_bias(pmod1, 2 * KT, DEPTH * NMOD)

            dve.wait_ge(vec_in, 16)
            lv = vec[:, V_LAM:V_LAM + 4 * DK].rearrange("p (a b) -> p a b", a=4)
            tt(lamp[:, :, :], lv[:, 0:4:2, :], lv[:, 1:4:2, :], ALU.mult)
            dve.drain()
            nc.vector.tensor_reduce(lam[:, 0:2], lamp[:, :, :], AX.X, ALU.add).then_inc(lam_prod, 1)
            ts(lam[:, 6:7], vec[:, V_SUB:V_SUB + 1], 1.0 - LAM_INIT, None, ALU.mult)
            for j in range(KT):
                clear_pads(O32[:, j, :])
            dve.wait_ge(lam_exp, 1)
            stt(out=lam[:, 4:5], in0=lam[:, 3:4], scalar=-LAM_INIT, in1=lam[:, 2:3], op0=ALU.add, op1=ALU.subtract)
            dve.drain()

            def nmax(idx, i):
                dve.wait_ge(sc_done, idx + 1)
                w = CTX if i == 4 else LAT + PAST
                s_ = psS[:, 0:2 * (LAT + PAST)].rearrange("p (m k) -> p m k", m=2)[:, :, 0:w]
                nc.vector.tensor_reduce(sm[:, 0:2], s_, AX.X, ALU.max)
                dve.drain()
                ts(sm[:, 2:4], sm[:, 0:2], -QSCALE, None, ALU.mult).then_inc(nmax_ready, 1)

            def combine(idx, i):
                w = CTX if i == 4 else LAT + PAST
                dve.wait_ge(exp_ready, idx + 1)
                nc.vector.reciprocal(sm[:, 6:8], sm[:, 4:6])
                dve.drain()
                tt(sm[:, 8:9], sm[:, 7:8], lam[:, 4:5], ALU.mult)
                ts(pr[:, 0, 0:w], pr[:, 0, 0:w], sm[:, 6:7], None, ALU.mult)
                dve.drain()
                stt(out=pr[:, 0, 0:w], in0=pr[:, 1, 0:w], scalar=sm[:, 8:9], in1=pr[:, 0, 0:w], op0=ALU.mult,
                    op1=ALU.add).then_inc(att_ready, 1)

            def turned(idx, i):
                dve.wait_ge(at_hi, idx + 1)
                if i == 4:
                    tt(Apl[:, :], psT[:, 0, 0:CTX], Aph[:, :].bitcast(F32), ALU.subtract).then_inc(t_free, 1)
                else:
                    t = psT[:, :, :].rearrange("p a b -> p (a b)")[:, 0:5 * P].rearrange("p (c q) -> p c q", c=5)
                    tt(Al[:, :, i * P:(i + 1) * P], t, Ah[:, :, i * P:(i + 1) * P].bitcast(F32), ALU.subtract).then_inc(t_free, 1)

            def rotate(use, src):
                dve.wait_ge(t_full, use + 1)
                tt(sx[:, 0:LAT], psT[:, 0, :], rope[:, 1, :], ALU.mult).then_inc(t_free, 1)
                x = src[:, L0:L0 + LAT]
                tt(x, x, rope[:, 0, :], ALU.mult)
                dve.drain()
                tt(x, x, sx[:, 0:LAT], ALU.add).then_inc(roped, 1)
                dve.drain()

            def q_lo(n, par):
                dve.wait_ge(qk_hi, 2 * n + 1)
                tt(Ql[par][:, :], h32[0][:, :], Qh[par][:, :].bitcast(F32), ALU.subtract).then_inc(qk_ready, 1)

            def k_lo(n, par):
                dve.wait_ge(ckc_hi, n + 1)
                tt(Kl[par][:, L0 + LAT:KW], ckv[:, 0, :], Kh[par][:, L0 + LAT:KW].bitcast(F32), ALU.subtract)
                tt(Vl[par][:, 4, :], ckv[:, 1, :], Vh[par][:, 4, :].bitcast(F32), ALU.subtract).then_inc(ck_split, 1)
                dve.wait_ge(qk_hi, 2 * n + 2)
                tt(Kl[par][:, 0:L0 + LAT], h32[1][:, 0:L0 + LAT], Kh[par][:, 0:L0 + LAT].bitcast(F32),
                   ALU.subtract).then_inc(qk_ready, 1)

            def values_lo(n, par):
                dve.wait_ge(v_hi, n + 1)
                t = psT[:, :, :].rearrange("p a b -> p (a b)")[:, 0:5 * P].rearrange("p (c q) -> p c q", c=5)
                tt(Vl[par][:, 0:4, :], t[:, 0:4, :], Vh[par][:, 0:4, :].bitcast(F32), ALU.subtract)
                tt(Vl[par][:, 5, :], t[:, 4, :], Vh[par][:, 5, :].bitcast(F32), ALU.subtract).then_inc(t_free, 1)

            def step(m, par, last=False):
                h = 2 * m + par
                u = 3 + 9 * h
                n = h + 1
                e = 0 if last else 1
                for i, k in ((4, 0), (0, 1), (1, 2)):
                    nmax(5 * h + k, i)
                    combine(5 * h + k, i)
                    turned(5 * h + k, i)
                nmax(5 * h + 3, 2)
                if not last:
                    rotate(u + 3, h32[0])
                combine(5 * h + 3, 2)
                if not last:
                    q_lo(n, 1 - par)
                turned(5 * h + 3, 2)
                nmax(5 * h + 4, 3)
                combine(5 * h + 4, 3)
                turned(5 * h + 4, 3)
                if not last:
                    rotate(u + 6, h32[1])
                    k_lo(n, 1 - par)
                dve.wait_ge(t_free, u + 6 + 2 * e)
                nc.vector.reciprocal(rs[:, :, :], rs[:, :, :])
                dve.drain()
                ot = O32[:, bass.ds(h, 1), :].rearrange("p a t -> p (a t)") if not isinstance(h, int) else O32[:, h, :]
                stt(out=ot, in0=ot, scalar=lam[:, 6:7], in1=rs[:, :, :].rearrange("p a b -> p (a b)"), op0=ALU.mult,
                    op1=ALU.mult).then_inc(onorm, 1)
                if not last:
                    values_lo(n, 1 - par)

            dve.wait_ge(rope_in, 16)
            rotate(0, h32[0])
            q_lo(0, 0)
            rotate(1, h32[1])
            k_lo(0, 0)
            values_lo(0, 0)
            step(0, 0)
            step(0, 1)
            with dve.Fori(1, DA_HEADS // 2 - 1) as m:
                step(m, 0)
                step(m, 1)
            step(DA_HEADS // 2 - 1, 0)
            step(DA_HEADS // 2 - 1, 1, last=True)
            coefficients((0, 0), mod(0, 3), mod(0, 4))
            gated(U_WO, 2 * KT, 2, True, 0)
            for w in range(2):
                dve.wait_ge(kv_out[w], 16 * DA_HEADS)
            layer_norm(0)
            h_build(2)
            ffn(0, U_FFN0)
            layer_norm(1)
            coefficients((0, 1), mod(1, 0), mod(1, 1))
            h_build(3)

            nc.vector.memset(vc[:, MDV:MDV + 2], 1.0)
            nc.vector.memset(msm[:, 22:24], 0.0)
            nc.vector.memset(mask[:, 0:3 * P], 0.0)
            nc.vector.memset(mask[:, 5 * P:8 * P], 0.0)
            dve.wait_ge(tri_in, 32)
            nc.vector.memset(sx[:, 0:1], 0.0)
            nc.vector.memset(sx[:, TP + 1:TP + 2], 0.0)
            for j in range(2):
                clear_pads(hO[:, j, :])
            dve.wait_ge(wgh_ready, 1)
            tt(wgl[:, :, :], wgf[:, :, :], wgh[:, :, :].bitcast(F32), ALU.subtract).then_inc(wg_ready, 1)
            ts(mKh[:, TP - 2:TP - 2 + P], ident[:, :], 1.0, None, ALU.mult)
            ts(mKl[:, TP - 2:TP - 2 + P], ident[:, :], 0.0, None, ALU.mult)
            dve.wait_ge(mt_full, 1)
            bg = vec[:, V_BG:V_BG + 16]
            g5 = mT[:, 0, 0:80].rearrange("p (i g) -> p i g", i=5)
            tt(gt[:, :, :], g5, bg[:, None, :].to_broadcast([P, 5, 16]), ALU.add)
            dve.drain()
            gv = gt[:, :, :].rearrange("p i (d g h) -> p i d g h", d=2, g=2)
            for d in range(2):
                nc.vector.tensor_copy(xf[:, :, 4 * d:4 * d + 4], gv[:, :, d, 1, :])
            dve.drain()
            xff = xf[:, :, :].rearrange("p i c -> p (i c)")
            stt(out=lft[:, :], in0=xff, scalar=-1.0, in1=xff, op0=ALU.mult, op1=ALU.max).then_inc(ax_ready, 1)
            dve.wait_ge(ln_ready, 1)
            stt(out=lf[:, :, :].rearrange("p i c -> p (i c)"), in0=xff, scalar=0.0, in1=lft[:, :], op0=ALU.min,
                op1=ALU.subtract).then_inc(lf_ready, 1)
            dve.wait_ge(mt_full, 2)
            nc.vector.tensor_copy(bs[:, :], mT[:, 1, 0:48])
            dve.drain()
            bv = bs[:, 0:40].rearrange("p (i c) -> p i c", i=5)
            for d in range(2):
                last = tt(a5[:, :, 4 * d:4 * d + 4], gv[:, :, d, 0, :], bv[:, :, 4 * d:4 * d + 4], ALU.subtract)
            last.then_inc(mt_free, 2)
            dve.drain()

            def h_cols(t, h):
                return t.rearrange("p (d h) -> p d h", d=2)[:, :, bass.ds(h, 1)].rearrange("p d a -> p (d a)")

            def m_max(n, i):
                for d in range(2):
                    if i == 4:
                        w = (0, P)
                        src, mk = ab[:, d, 4 * P:5 * P], mask[:, (3 + d) * P:(4 + d) * P]
                    elif d == 0:
                        w = (0, (i + 1) * P)
                        src, mk = ab[:, 0, 0:w[1]], mask[:, (3 - i) * P:4 * P]
                    else:
                        w = (i * P, LAT)
                        src, mk = ab[:, 1, w[0]:w[1]], mask[:, 4 * P:4 * P + LAT - i * P]
                    tt(mW[:, d, w[0]:w[1]], src, mk, ALU.add)
                    dve.drain()
                    nc.vector.tensor_reduce(msm[:, d:d + 1], mW[:, d, w[0]:w[1]], AX.X, ALU.max)
                m0 = msm[:, 22:24] if i == 4 else msm[:, 18:20]
                dve.drain()
                tt(msm[:, 0:2], msm[:, 0:2], m0, ALU.max)
                dve.drain()
                ts(msm[:, 2:4], msm[:, 0:2], -1.0, None, ALU.mult)
                tt(msm[:, 4:6], m0, msm[:, 0:2], ALU.subtract)
                dve.drain()
                tt(msm[:, 6:8], msm[:, 2:4], bh[:, i, :], ALU.subtract).then_inc(mm_ready, 1)

            def m_combine(h, s, i):
                n = 5 * h + s
                dve.wait_ge(me_ready, n + 1)
                dve.wait_ge(ms_done, n + 1)
                w = [(0, P), (0, P)] if i == 4 else [(0, (i + 1) * P), (i * P, LAT)]
                for d in range(2):
                    a_, b_ = w[d]
                    stt(out=mW[:, d, a_:b_], in0=mS[:, 0, a_:b_], scalar=1.0, in1=mW[:, d, a_:b_], op0=ALU.mult, op1=ALU.mult,
                        accum_out=mdn[:, d:d + 1])
                dve.drain()
                if i < 4:
                    tt(mdn[:, 2:4], msm[:, 8:10], mS[:, 1, P:P + 2], ALU.mult)
                    dve.drain()
                    tt(mdn[:, 0:2], mdn[:, 0:2], mdn[:, 2:4], ALU.add)
                    dve.drain()
                stt(out=mdn[:, 4:6], in0=mdn[:, 0:2], scalar=-1.0, in1=mdn[:, 0:2], op0=ALU.mult, op1=ALU.max)
                dve.drain()
                tt(mdn[:, 4:6], mdn[:, 4:6], msm[:, 10:12], ALU.max)
                dve.drain()
                nc.vector.reciprocal(mdn[:, 6:8], mdn[:, 4:6])
                dve.drain()
                if i < 4:
                    tt(mdn[:, 8:10], mdn[:, 6:8], msm[:, 8:10], ALU.mult)
                    dve.drain()
                    for d in range(2):
                        ts(mA[:, (4 + d) * P:(5 + d) * P], mS[:, 1, 0:P], mdn[:, 8 + d:9 + d], None, ALU.mult)
                    if i < 3:
                        ts(mA[:, (i + 1) * P:LAT], mW[:, 1, (i + 1) * P:LAT], mdn[:, 7:8], None, ALU.mult)
                d0 = 0 if i == 4 else i * P
                ts(mA[:, 0:d0 + P], mW[:, 0, 0:d0 + P], mdn[:, 6:7], None, ALU.mult)
                dve.drain()
                stt(out=mA[:, d0:d0 + P], in0=mW[:, 1, d0:d0 + P], scalar=mdn[:, 7:8], in1=mA[:, d0:d0 + P], op0=ALU.mult,
                    op1=ALU.add).then_inc(ma_ready, 1)
                dve.drain()

            def m_turned(h, s, i):
                dve.wait_ge(mat_hi, 5 * h + s + 1)
                t = mT[:, :, :].rearrange("p a b -> p (a b)")
                if i == 4:
                    tt(mApl[:, :], t[:, 0:P], mAph[:, :].bitcast(F32), ALU.subtract).then_inc(mt_free, 1)
                else:
                    c = (i % 2) * P
                    tt(mAl[:, :, c:c + P], t[:, 0:6 * P].rearrange("p (c q) -> p c q", c=6),
                       mAh[:, :, c:c + P].bitcast(F32), ALU.subtract).then_inc(mt_free, 1)

            def m_conv(h, w):
                dve.wait_ge(pj_copied, MCOP + 6 * h + w + 1)
                c = h32[w]
                tap = [col(V_MCW + KT * t + 4 * w + h) for t in range(3)]
                ts(c[:, :], sx[:, 1:TP + 1], tap[1], col(V_MCB + 4 * w + h), ALU.mult, ALU.add)
                dve.drain()
                stt(out=c[:, :], in0=sx[:, 0:TP], scalar=tap[0], in1=c[:, :], op0=ALU.mult, op1=ALU.add)
                dve.drain()
                stt(out=c[:, :], in0=sx[:, 2:TP + 2], scalar=tap[2], in1=c[:, :], op0=ALU.mult,
                    op1=ALU.add).then_inc(mconv, 1)

            def m_head(h):
                u = 2 + 13 * h
                for d in range(2):
                    c = 4 * d
                    nc.vector.tensor_copy(ah[:, :, d:d + 1], a5[:, :, bass.ds(c + h, 1)])
                    nc.vector.tensor_copy(bh[:, :, d:d + 1], bv[:, :, bass.ds(c + h, 1)])
                nc.vector.tensor_copy(msm[:, 18:20], h_cols(vec[:, V_M0:V_M0 + 8], h))
                nc.vector.tensor_copy(msm[:, 20:22], h_cols(vec[:, V_N0:V_N0 + 8], h))
                dve.drain()
                for d in range(2):
                    if d == 1:
                        dve.wait_ge(mt_full, u + 1)
                    tt(dg[:, :, :], ident[:, None, :].to_broadcast([P, 5, P]), ah[:, :, d:d + 1].to_broadcast([P, 5, P]),
                       ALU.mult).then_inc(dg_ready, 1)
                m_conv(h, 0)
                dve.drain()
                dve.wait_ge(msilu, 2 * h + 1)
                m_conv(h, 1)
                dve.wait_ge(mq_hi, 2 * h + 1)
                tt(mQl[:, :], h32[0][:, :], mQh[:, :].bitcast(F32), ALU.subtract)
                dve.drain()
                dve.wait_ge(mt_free, u + 2)
                m_max(5 * h, 4)
                dve.wait_ge(msilu, 2 * h + 2)
                ts(h32[1][:, :], h32[1][:, :], KSCALE, None, ALU.mult).then_inc(mk_scaled, 1)
                dve.drain()
                dve.wait_ge(mq_hi, 2 * h + 2)
                tt(mKl[:, TP - 2 + P:TP + P], msm[:, 20:22], mKh[:, TP - 2 + P:TP + P].bitcast(F32), ALU.subtract)
                tt(mKl[:, 0:TP - 2], h32[1][:, 0:TP - 2], mKh[:, 0:TP - 2].bitcast(F32), ALU.subtract).then_inc(mk_ready, 1)
                m_combine(h, 0, 4)
                m_max(5 * h + 1, 0)
                m_turned(h, 0, 4)
                nc.vector.tensor_reduce(msm[:, 12:14], ab[:, :, 4 * P:5 * P], AX.X, ALU.max)
                dve.drain()
                ts(msm[:, 12:14], msm[:, 12:14], 0.0, None, ALU.max)
                dve.drain()
                tt(msm[:, 14:16], ah[:, 4, :], msm[:, 12:14], ALU.subtract).then_inc(dw_ready, 1)
                tt(mst[:, :, bass.ds(h, 1)].rearrange("p d a -> p (d a)"), msm[:, 12:14], h_cols(bs[:, 40:48], h), ALU.add)
                for w in range(2):
                    dve.wait_ge(mv_hi, 2 * h + w + 1)
                    t = mT[:, :, :].rearrange("p a b -> p (a b)")[:, 0:5 * P].rearrange("p (c q) -> p c q", c=5)
                    tt(mVl[:, :, w * P:(w + 1) * P], t, mVh[:, :, w * P:(w + 1) * P].bitcast(F32), ALU.subtract).then_inc(mt_free, 1)
                dve.wait_ge(mc_hi, h + 1)
                tt(mCl[:, :, :], c0[:, :, :], mCh[:, :, :].bitcast(F32), ALU.subtract).then_inc(c0_split, 1)
                m_combine(h, 1, 0)
                m_max(5 * h + 2, 1)
                m_turned(h, 1, 0)
                m_combine(h, 2, 1)
                m_max(5 * h + 3, 2)
                m_turned(h, 2, 1)
                dve.wait_ge(mt_full, u + 8)
                dve.wait_ge(ws_ready, h + 1)
                for d in range(2):
                    last = ts(kw[:, d, :], mT[:, 0, 0:P], msm[:, 16 + d:17 + d], None, ALU.mult)
                last.then_inc(mt_free, 1)
                m_combine(h, 3, 2)
                m_max(5 * h + 4, 3)
                m_turned(h, 3, 2)
                m_combine(h, 4, 3)
                m_turned(h, 4, 3)
                dve.wait_ge(mt_full, u + 12)
                for w in range(2):
                    x = hO[:, w, :].rearrange("p (a b) -> p a b", a=2)
                    last = stt(out=x, in0=mT[:, :, 0:HALF], scalar=-1.0 / MDV, in1=x, op0=ALU.mult, op1=ALU.add)
                last.then_inc(mt_free, 1)
                dve.wait_ge(mt_free, u + 13)
                nc.vector.reciprocal(rs[:, :, :], rs[:, :, :])
                dve.drain()
                for w in range(2):
                    stt(out=hO[:, w, :], in0=hO[:, w, :], scalar=col(V_MNW + 2 * h + w), in1=rs[:, :, :].rearrange("p a b -> p (a b)"),
                        op0=ALU.mult, op1=ALU.mult)
                dve.drain()
                for w in range(2):
                    last = tt(O32m[:, bass.ds(2 * h + w, 1), :].rearrange("p a t -> p (a t)"), hO[:, w, :], sig[:, w, :], ALU.mult)
                last.then_inc(mout_done, 1)
                dve.drain()

            m_head(0)
            with dve.Fori(1, ML_HEADS) as h:
                m_head(h)
            dve.wait_ge(x_ready, 2 * KT)
            coefficients((1, 0), mod(1, 3), mod(1, 4))
            gated(U_MLOUT, NMOD + 2 * KT, 2, True, 0)
            layer_norm(2)
            dve.wait_ge(c_out, 32 * ML_HEADS)
            h_build(5)
            ffn(1, U_FFN1)
            coefficients((1, 1))
            layer_norm(3)
            for j in range(KT):
                ts(X[:, j, :], X[:, j, :], xa[:, j:j + 1], xb[:, j:j + 1], ALU.mult, ALU.add).then_inc(y_ready, 1)


def _rope_tables():
    nf = DK // 4
    inv = (np.float32(10000.0) ** (-np.arange(nf, dtype=np.float32) / np.float32(nf))).astype(np.float32)
    tok = np.arange(LAT)
    pos = np.stack([tok // GRID_W, tok % GRID_W]).astype(np.float32)
    t = np.zeros((P, 2, LAT), np.float32)
    for p in range(P):
        d = p % DK
        ang = pos[d // (2 * nf)] * inv[d % nf]
        t[p, 0] = np.cos(ang)
        t[p, 1] = np.sin(ang) * (-1.0 if d % (2 * nf) < nf else 1.0)
    return t


def _matrices():
    i = np.arange(P)
    m = np.zeros((P, 6, P), np.float32)
    m[i, 0, i] = 1.0
    m[i, 1, i ^ (DK // 4)] = 1.0
    m[:, 2] = i[:, None] <= i[None, :]
    m[:, 3] = i[:, None] >= i[None, :]
    m[:, 4] = np.where(i[None, :] <= i[:, None], 0.0, -1e30)
    m[:, 5] = np.where(i[None, :] >= i[:, None], 0.0, -1e30)
    return m


def _units(w, tiles, kt):
    return np.ascontiguousarray(w.reshape(kt, P, -1, P).transpose(2, 1, 0, 3)[tiles].reshape(len(tiles), P, kt * P))


def _layout(x):
    xT = np.zeros((P, KT, TP), np.float32)
    feat = lambda t: t.T.reshape(KT, P, -1).transpose(1, 0, 2)
    xT[:, :, C0:C0 + CTX] = feat(x["x_prompt"][0])
    xT[:, :, L0:L0 + LAT] = feat(x["x_sample"][0])
    cols = lambda v: v.reshape(-1, P).T
    order = [[t for j in range(h * GH, (h + 1) * GH) for t in (j, 2 * GH + j)] for h in range(2)]
    pick = lambda v, h: cols(v)[:, order[h]]
    fcw, fcb = x["ffn_conv_w"], x["ffn_conv_b"]
    rows = lambda v: np.broadcast_to(v.reshape(1, -1), (P, v.size))
    vec = [cols(x["ada_b"])] + [cols(x["ln_g"]), cols(x["ln_b"])]
    vec += [pick(fcw[l, t], h) for l in range(DEPTH) for h in range(2) for t in range(3)]
    vec += [pick(fcb[l], h) for l in range(DEPTH) for h in range(2)]
    vec += [cols(x["ml_conv_w"][0]), cols(x["ml_conv_b"][0]), cols(x["da_subln"][0]), cols(x["ml_norm_w"][0])]
    vec += [x["state_n"][0, 0].reshape(-1, MDK).T, rows(x["state_m"][0, 0]), rows(x["ml_b_gate"][0]), rows(x["da_lam"][0])]
    vec += [np.stack([cols(x["c_ctx"]), cols(x["c"][0])], axis=-1).reshape(P, 2 * KT)]
    vecs = np.ascontiguousarray(np.concatenate(vec, axis=1))
    assert vecs.shape[1] == NV, (vecs.shape, NV)
    heads = [t for h in range(DA_HEADS) for t in (h, DA_HEADS + h, 2 * DA_HEADS + h)]
    mlin = [t for h in range(ML_HEADS) for t in (h, ML_HEADS + h, 8 + 2 * h, 9 + 2 * h, 16 + 2 * h, 17 + 2 * h)]
    wm = x["ml_w_in"][0]
    return {
        "xT": xT, "vecs": vecs, "mats": _matrices(), "rope": _rope_tables(),
        "w_ada": np.ascontiguousarray(x["ada_w"].reshape(DEPTH, KT // 2, 2, P, NMOD // 4, 512).transpose(
            0, 4, 1, 3, 2, 5)).reshape(DEPTH * NMOD, P, 2 * 512),
        "w_qkv": _units(x["da_w_qkv"][0], heads, KT),
        "w_wo": _units(x["da_w_o"][0], list(range(KT)), KT),
        "w_up": np.concatenate([_units(x["ffn_w_up"][l], order[h], KT) for l in range(DEPTH) for h in range(2)]),
        "w_dn": np.concatenate([_units(x["ffn_w_down"][l][h * WMAX:(h + 1) * WMAX], list(range(KT)), GH)
                                for l in range(DEPTH) for h in range(2)]),
        "w_mlin": _units(np.ascontiguousarray(wm[:, :3072]), mlin, KT),
        "w_gate": np.ascontiguousarray(wm[:, 3072:].reshape(KT, P, 16).transpose(1, 0, 2)),
        "w_mlout": _units(x["ml_w_out"][0], list(range(KT)), KT),
        "cache_kT": np.ascontiguousarray(x["cache_k"][0, 0].reshape(PAST, DA_HEADS, P).transpose(1, 2, 0)),
        "cache_v": np.ascontiguousarray(x["cache_v"][0, 0].transpose(1, 0, 2)),
        "state_C": np.ascontiguousarray(x["state_C"][0, 0].transpose(2, 1, 0, 3)),
    }


_OUTS = {"yT": (P, KT, TP), "cache_kT": (DA_HEADS, P, CTX), "cache_vT": (DA_HEADS, P, CTX),
         "state_C": (2 * ML_HEADS, P, MDV), "state_n": (P, 2 * ML_HEADS), "state_m": (2 * ML_HEADS,)}


def kernel(**inputs):
    import concourse.bacc as _bacc
    from concourse.bass_utils import run_bass_kernel_spmd as _run

    nc = _bacc.Bacc("TRN2", target_bir_lowering=False, num_devices=1)
    arrays = {f"in_{n}": v for n, v in _layout({n: np.asarray(v) for n, v in inputs.items()}).items()}
    a = {n[3:]: nc.dram_tensor(n, v.shape, F32, kind="ExternalInput").ap() for n, v in arrays.items()}
    o = {n: nc.dram_tensor(f"out_{n}", s, F32, kind="ExternalOutput").ap() for n, s in _OUTS.items()}
    hybrid_step(nc, a, o)
    r = _run(nc, [arrays], core_ids=[0]).results[0]
    y = r["out_yT"].transpose(2, 1, 0).reshape(TP, D)
    return (np.ascontiguousarray(y[None, C0:C0 + CTX]), np.ascontiguousarray(y[None, L0:L0 + LAT]),
            np.ascontiguousarray(r["out_cache_kT"].transpose(2, 0, 1)).reshape(1, 1, CTX, DA_HEADS, 2, DK),
            np.ascontiguousarray(r["out_cache_vT"].transpose(2, 0, 1)).reshape(1, 1, CTX, DA_HEADS, 2 * DK),
            r["out_state_C"].reshape(1, 1, 2, ML_HEADS, MDK, MDV), np.ascontiguousarray(r["out_state_n"].T).reshape(1, 1, 2, ML_HEADS, MDK),
            r["out_state_m"].reshape(1, 1, 2, ML_HEADS))
```
